# Optimizing a Trainium2 kernel written in Bass

```python
import jax, jax.numpy as jnp
from jax import lax
import numpy as np

D_MODEL = 1024
BATCH = 1
SEQ = 512
DEPTH = 2

GRID_W = 64
CTX_LEN = 256
HEAD_DIM = 64
Q_BLOCK = 128
ROPE_THETA = 10000.0
EPS = 1e-6
NEG = -1e30

A_HEADS = 4
A_KV_HEADS = 2
B_HEADS = 4
B_NOPE = 64
B_ROPE = 32
B_V = 64
B_KV_RANK = 128
C_HEADS = 4
C_KV_HEADS = 2
C_WINDOW = 128
D_HEADS = 4
NA_ROWS = 8
NA_COLS = 16
NA_QCOLS = 16
NA_KCOLS = NA_QCOLS + NA_COLS

N_EXPERTS = 64
TOP_K = 8
N_GROUPS = 8
TOPK_GROUPS = 4
EXPERT_DIM = 256
SHARED_DIM = 256
ROUTED_SCALE = 2.5
MOE_BLOCK = 128

A_Q = A_HEADS * HEAD_DIM
A_KV = A_KV_HEADS * HEAD_DIM
B_Q = B_HEADS * (B_NOPE + B_ROPE)
C_Q = C_HEADS * HEAD_DIM
C_KV = C_KV_HEADS * HEAD_DIM
D_QKV = D_HEADS * HEAD_DIM
IN_SPLITS = (A_Q, A_KV, A_KV, B_Q, B_KV_RANK, B_ROPE, C_Q, C_KV, C_KV, D_QKV, D_QKV, D_QKV)
IN_WIDTH = A_Q + 2 * A_KV + B_Q + B_KV_RANK + B_ROPE + C_Q + 2 * C_KV + 3 * D_QKV
MIX_WIDTH = A_HEADS * HEAD_DIM + B_HEADS * B_V + C_HEADS * HEAD_DIM + D_HEADS * HEAD_DIM

kernel_name = "hybrid_parallel_heads_moe_dit_block"

def _rms_norm(x, g):
    xf = x.astype(jnp.float32)
    y = xf * lax.rsqrt(jnp.mean(xf * xf, axis=-1, keepdims=True) + EPS)
    return (y * g.astype(jnp.float32)).astype(x.dtype)

def _axial_rope(n_tok, dim):
    t = jnp.arange(n_tok)
    row = (t // GRID_W).astype(jnp.float32)
    col = (t % GRID_W).astype(jnp.float32)
    quarter = dim // 4
    freqs = ROPE_THETA ** (-jnp.arange(quarter, dtype=jnp.float32) / quarter)
    ar = row[:, None] * freqs
    ac = col[:, None] * freqs
    ang = jnp.concatenate([ar, ar, ac, ac], axis=-1)
    return jnp.cos(ang), jnp.sin(ang)

def _rope(x, cos, sin):
    xf = x.astype(jnp.float32)
    x1, x2, x3, x4 = jnp.split(xf, 4, axis=-1)
    rot = jnp.concatenate([-x2, x1, -x4, x3], axis=-1)
    return (xf * cos + rot * sin).astype(x.dtype)

def _heads(x, n):
    b, t, _ = x.shape
    return x.reshape(b, t, n, -1).transpose(0, 2, 1, 3)

def _merge(x):
    b, h, t, d = x.shape
    return x.transpose(0, 2, 1, 3).reshape(b, t, h * d)

def _group(x, hk):
    b, h, t, d = x.shape
    return x.reshape(b, hk, h // hk, t, d)

def _ungroup(x):
    b, hk, g, t, d = x.shape
    return x.reshape(b, hk * g, t, d)

def _split_cols(p):
    offs, acc = [], 0
    for w in IN_SPLITS[:-1]:
        acc += w
        offs.append(acc)
    return jnp.split(p, offs, axis=-1)

def _dense_block_attn(q, k, v, scale):
    bsz, hk, g, sq, dk = q.shape
    nb = sq // Q_BLOCK
    qb = jnp.moveaxis(q.reshape(bsz, hk, g, nb, Q_BLOCK, dk), 3, 0)

    def one_block(qi):
        s = jnp.einsum("bhgqd,bhkd->bhgqk", qi, k, preferred_element_type=jnp.float32) * scale
        p = jax.nn.softmax(s, axis=-1).astype(v.dtype)
        return jnp.einsum("bhgqk,bhkd->bhgqd", p, v)

    o = lax.map(one_block, qb)
    return jnp.moveaxis(o, 0, 3).reshape(bsz, hk, g, sq, v.shape[-1])

def _ctx_attn(q, k, v, scale, sink=None):
    s = jnp.einsum("bhgqd,bhkd->bhgqk", q, k, preferred_element_type=jnp.float32) * scale
    if sink is not None:
        s_sink = jnp.broadcast_to(sink.astype(jnp.float32)[None, :, :, None, None], s.shape[:-1] + (1,))
        s = jnp.concatenate([s, s_sink], axis=-1)
    p = jax.nn.softmax(s, axis=-1)[..., :k.shape[2]].astype(v.dtype)
    return jnp.einsum("bhgqk,bhkd->bhgqd", p, v)

def _window_attn(q, k, v, kc, vc, sink, scale):
    bsz, hk, g, s_len, d = q.shape
    halo = -(-C_WINDOW // Q_BLOCK)
    nb = s_len // Q_BLOCK
    nkb = (2 * halo + 1) * Q_BLOCK
    pad = ((0, 0), (0, 0), (halo * Q_BLOCK, halo * Q_BLOCK), (0, 0))

    def band(t):
        tp = jnp.pad(t, pad).reshape(bsz, hk, nb + 2 * halo, Q_BLOCK, t.shape[-1])
        return jnp.concatenate([tp[:, :, j:j + nb] for j in range(2 * halo + 1)], axis=3)

    kb, vb = band(k), band(v)
    qb = q.reshape(bsz, hk, g, nb, Q_BLOCK, d)
    s_band = jnp.einsum("bhgnqd,bhnkd->bhgnqk", qb, kb, preferred_element_type=jnp.float32) * scale
    qpos = (jnp.arange(nb)[:, None] * Q_BLOCK + jnp.arange(Q_BLOCK))[:, :, None]
    kpos = (jnp.arange(nb)[:, None] * Q_BLOCK - halo * Q_BLOCK + jnp.arange(nkb))[:, None, :]
    valid = (kpos >= 0) & (kpos < s_len) & (jnp.abs(qpos - kpos) <= C_WINDOW)
    s_band = jnp.where(valid, s_band, NEG)
    s_ctx = jnp.einsum("bhgnqd,bhld->bhgnql", qb, kc, preferred_element_type=jnp.float32) * scale
    s_sink = jnp.broadcast_to(sink.astype(jnp.float32)[None, :, :, None, None, None], s_band.shape[:-1] + (1,))
    p = jax.nn.softmax(jnp.concatenate([s_band, s_ctx, s_sink], axis=-1), axis=-1)
    n_ctx = kc.shape[2]
    o = (jnp.einsum("bhgnqk,bhnkd->bhgnqd", p[..., :nkb].astype(v.dtype), vb)
         + jnp.einsum("bhgnql,bhld->bhgnqd", p[..., nkb:nkb + n_ctx].astype(vc.dtype), vc))
    return o.reshape(bsz, hk, g, s_len, d)

def _neighbourhood_attn(q, k, v, kc, vc, rpb, scale):
    bsz, nh, s_len, d = q.shape
    rows = s_len // GRID_W
    wr = min(NA_ROWS, rows)
    ncb = GRID_W // NA_QCOLS
    r = jnp.arange(rows)
    rs = jnp.clip(r - wr // 2, 0, rows - wr)
    key_rows = rs[:, None] + jnp.arange(wr)
    cb = jnp.arange(ncb)
    c0 = jnp.clip(cb * NA_QCOLS - NA_COLS // 2, 0, GRID_W - NA_KCOLS)
    key_cols = c0[:, None] + jnp.arange(NA_KCOLS)
    nk = wr * NA_KCOLS
    key_idx = (key_rows[:, None, :, None] * GRID_W + key_cols[None, :, None, :]).reshape(rows, ncb, nk)
    kg = jnp.take(k, key_idx, axis=2)
    vg = jnp.take(v, key_idx, axis=2)
    qb = q.reshape(bsz, nh, rows, ncb, NA_QCOLS, d)
    s_nb = jnp.einsum("bhrcqd,bhrckd->bhrcqk", qb, kg, preferred_element_type=jnp.float32) * scale
    q_cols = cb[:, None] * NA_QCOLS + jnp.arange(NA_QCOLS)
    q_cs = jnp.clip(q_cols - NA_COLS // 2, 0, GRID_W - NA_COLS)
    kcol = key_cols[:, None, :]
    col_ok = (kcol >= q_cs[:, :, None]) & (kcol < q_cs[:, :, None] + NA_COLS)
    mask = jnp.broadcast_to(col_ok[:, :, None, :], (ncb, NA_QCOLS, wr, NA_KCOLS)).reshape(ncb, NA_QCOLS, nk)
    dr = key_rows - r[:, None] + NA_ROWS - 1
    dc = jnp.clip(kcol - q_cols[:, :, None] + NA_COLS - 1, 0, 2 * NA_COLS - 2)
    bias = rpb[:, dr[:, None, None, :, None], dc[None, :, :, None, :]]
    bias = bias.reshape(nh, rows, ncb, NA_QCOLS, nk).astype(jnp.float32)
    s_nb = jnp.where(mask, s_nb + bias, NEG)
    s_ctx = jnp.einsum("bhrcqd,bhld->bhrcql", qb, kc, preferred_element_type=jnp.float32) * scale
    p = jax.nn.softmax(jnp.concatenate([s_nb, s_ctx], axis=-1), axis=-1)
    o = (jnp.einsum("bhrcqk,bhrckd->bhrcqd", p[..., :nk].astype(v.dtype), vg)
         + jnp.einsum("bhrcql,bhld->bhrcqd", p[..., nk:].astype(vc.dtype), vc))
    return o.reshape(bsz, nh, s_len, d)

def _mixer_full_gqa(q, k, v, qc, kc, vc, q_gain, k_gain, cos, sin, with_ctx):
    scale = HEAD_DIM ** -0.5
    bsz, s_len, _ = q.shape
    ql = _rope(_rms_norm(_heads(q, A_HEADS), q_gain), cos, sin)
    kl = _rope(_rms_norm(_heads(k, A_KV_HEADS), k_gain), cos, sin)
    kcx = _rms_norm(_heads(kc, A_KV_HEADS), k_gain)
    vl, vcx = _heads(v, A_KV_HEADS), _heads(vc, A_KV_HEADS)
    o = _dense_block_attn(_group(ql, A_KV_HEADS), jnp.concatenate([kl, kcx], axis=2),
                          jnp.concatenate([vl, vcx], axis=2), scale)
    out = _merge(_ungroup(o))
    out_c = None
    if with_ctx:
        qcx = _rms_norm(_heads(qc, A_HEADS), q_gain)
        out_c = _merge(_ungroup(_ctx_attn(_group(qcx, A_KV_HEADS), kcx, vcx, scale)))
    return out, out_c

def _mixer_mla(q, ckv, kr, qc, ckvc, krc, kv_gain, w_kv_up, cos, sin, with_ctx):
    scale = (B_NOPE + B_ROPE) ** -0.5

    def expand(c_lat, k_rope):
        kv = _heads(_rms_norm(c_lat, kv_gain) @ w_kv_up, B_HEADS)
        kr_h = jnp.broadcast_to(k_rope[:, None], kv.shape[:-1] + (B_ROPE,))
        return jnp.concatenate([kv[..., :B_NOPE], kr_h], axis=-1), kv[..., B_NOPE:]

    kl, vl = expand(ckv, _rope(kr, cos, sin))
    kcx, vcx = expand(ckvc, krc)
    qh = _heads(q, B_HEADS)
    ql = jnp.concatenate([qh[..., :B_NOPE], _rope(qh[..., B_NOPE:], cos, sin)], axis=-1)
    o = _dense_block_attn(ql[:, :, None], jnp.concatenate([kl, kcx], axis=2),
                          jnp.concatenate([vl, vcx], axis=2), scale)
    out = _merge(o[:, :, 0])
    out_c = None
    if with_ctx:
        out_c = _merge(_ctx_attn(_heads(qc, B_HEADS)[:, :, None], kcx, vcx, scale)[:, :, 0])
    return out, out_c

def _mixer_window_gqa(q, k, v, qc, kc, vc, sink, cos, sin, with_ctx):
    scale = HEAD_DIM ** -0.5
    sink_g = sink.reshape(C_KV_HEADS, C_HEADS // C_KV_HEADS)
    ql = _rope(_heads(q, C_HEADS), cos, sin)
    kl = _rope(_heads(k, C_KV_HEADS), cos, sin)
    vl = _heads(v, C_KV_HEADS)
    kcx, vcx = _heads(kc, C_KV_HEADS), _heads(vc, C_KV_HEADS)
    out = _merge(_ungroup(_window_attn(_group(ql, C_KV_HEADS), kl, vl, kcx, vcx, sink_g, scale)))
    out_c = None
    if with_ctx:
        qcx = _group(_heads(qc, C_HEADS), C_KV_HEADS)
        out_c = _merge(_ungroup(_ctx_attn(qcx, kcx, vcx, scale, sink_g)))
    return out, out_c

def _mixer_neighbourhood(q, k, v, qc, kc, vc, rpb, with_ctx):
    scale = HEAD_DIM ** -0.5
    kcx, vcx = _heads(kc, D_HEADS), _heads(vc, D_HEADS)
    out = _merge(_neighbourhood_attn(_heads(q, D_HEADS), _heads(k, D_HEADS), _heads(v, D_HEADS),
                                     kcx, vcx, rpb, scale))
    out_c = None
    if with_ctx:
        out_c = _merge(_ctx_attn(_heads(qc, D_HEADS)[:, :, None], kcx, vcx, scale)[:, :, 0])
    return out, out_c

def _route(h, w_r, b_r):
    s = jax.nn.sigmoid(jnp.matmul(h, w_r, preferred_element_type=jnp.float32))
    sb = s + b_r.astype(jnp.float32)
    n_tok = s.shape[0]
    per = N_EXPERTS // N_GROUPS
    gscore = lax.top_k(sb.reshape(n_tok, N_GROUPS, per), 2)[0].sum(-1)
    _, gidx = lax.top_k(gscore, TOPK_GROUPS)
    gmask = jnp.sum(jax.nn.one_hot(gidx, N_GROUPS, dtype=jnp.float32), axis=1)
    emask = jnp.repeat(gmask, per, axis=1) > 0
    _, idx = lax.top_k(jnp.where(emask, sb, -jnp.inf), TOP_K)
    w = jnp.take_along_axis(s, idx, axis=1)
    w = w / jnp.sum(w, axis=-1, keepdims=True) * ROUTED_SCALE
    return idx, w

def _swiglu(x, wg, wu, wd):
    return (jax.nn.silu(x @ wg) * (x @ wu)) @ wd

def _moe_routed(h, idx, wts, wg, wu, wd):
    n_tok, dm = h.shape
    n_asg = n_tok * TOP_K
    flat_e = idx.reshape(-1)
    order = jnp.argsort(flat_e)
    sorted_e = flat_e[order]
    counts = jnp.bincount(flat_e, length=N_EXPERTS)
    padded = (counts + MOE_BLOCK - 1) // MOE_BLOCK * MOE_BLOCK
    pad_end = jnp.cumsum(padded)
    pad_start = pad_end - padded
    raw_start = jnp.cumsum(counts) - counts
    slot = pad_start[sorted_e] + jnp.arange(n_asg) - raw_start[sorted_e]
    n_blocks = -(-(n_asg + N_EXPERTS * (MOE_BLOCK - 1)) // MOE_BLOCK)
    n_slots = n_blocks * MOE_BLOCK
    slot_tok = jnp.full((n_slots,), n_tok, jnp.int32).at[slot].set((order // TOP_K).astype(jnp.int32))
    slot_w = jnp.zeros((n_slots,), wts.dtype).at[slot].set(wts.reshape(-1)[order])
    block_e = jnp.minimum(jnp.searchsorted(pad_end, jnp.arange(n_blocks) * MOE_BLOCK, side="right"),
                          N_EXPERTS - 1)
    h_pad = jnp.concatenate([h, jnp.zeros((1, dm), h.dtype)], axis=0)

    def step(acc, blk):
        tok, w, e = blk
        xb = h_pad[tok]
        y = (jax.nn.silu(xb @ wg[e]) * (xb @ wu[e])) @ wd[e]
        return acc.at[tok].add(y * w[:, None].astype(y.dtype)), None

    acc, _ = lax.scan(step, jnp.zeros((n_tok + 1, dm), h.dtype),
                      (slot_tok.reshape(n_blocks, MOE_BLOCK), slot_w.reshape(n_blocks, MOE_BLOCK), block_e))
    return acc[:n_tok]

def _moe(h, w_r, b_r, wg, wu, wd, swg, swu, swd):
    idx, wts = _route(h, w_r, b_r)
    return _moe_routed(h, idx, wts, wg, wu, wd) + _swiglu(h, swg, swu, swd)

def setup_inputs(seed: int = 0) -> dict:
    key = jax.random.key(seed)
    ks = jax.random.split(key, 32)
    f32 = jnp.float32
    L = DEPTH

    def nrm(k, shape, scale):
        return jax.random.normal(k, shape, f32) * scale

    return {
        "x": nrm(ks[0], (BATCH, SEQ, D_MODEL), 1.0),
        "c": nrm(ks[1], (BATCH, D_MODEL), 1.0),
        "ctx": nrm(ks[2], (BATCH, CTX_LEN, D_MODEL), 1.0),
        "c_ctx": nrm(ks[3], (D_MODEL,), 1.0),
        "ada_w": nrm(ks[4], (L, D_MODEL, 6 * D_MODEL), 0.5 * D_MODEL ** -0.5),
        "ada_b": nrm(ks[5], (L, 6 * D_MODEL), 0.01),
        "pre_mix_g": 1.0 + nrm(ks[6], (L, D_MODEL), 0.1),
        "post_mix_g": 1.0 + nrm(ks[7], (L, D_MODEL), 0.1),
        "pre_ffn_g": 1.0 + nrm(ks[8], (L, D_MODEL), 0.1),
        "post_ffn_g": 1.0 + nrm(ks[9], (L, D_MODEL), 0.1),
        "w_in": nrm(ks[10], (L, D_MODEL, IN_WIDTH), D_MODEL ** -0.5),
        "a_q_norm": 1.0 + nrm(ks[11], (L, HEAD_DIM), 0.1),
        "a_k_norm": 1.0 + nrm(ks[12], (L, HEAD_DIM), 0.1),
        "b_kv_norm": 1.0 + nrm(ks[13], (L, B_KV_RANK), 0.1),
        "b_w_kv_up": nrm(ks[14], (L, B_KV_RANK, B_HEADS * (B_NOPE + B_V)), B_KV_RANK ** -0.5),
        "c_sink": nrm(ks[15], (L, C_HEADS), 1.0),
        "d_rpb": nrm(ks[16], (L, D_HEADS, 2 * NA_ROWS - 1, 2 * NA_COLS - 1), 0.2),
        "w_out": nrm(ks[17], (L, MIX_WIDTH, D_MODEL), MIX_WIDTH ** -0.5),
        "router_w": nrm(ks[18], (L, D_MODEL, N_EXPERTS), D_MODEL ** -0.5),
        "router_b": nrm(ks[19], (L, N_EXPERTS), 0.01),
        "exp_w_gate": nrm(ks[20], (L, N_EXPERTS, D_MODEL, EXPERT_DIM), D_MODEL ** -0.5),
        "exp_w_up": nrm(ks[21], (L, N_EXPERTS, D_MODEL, EXPERT_DIM), D_MODEL ** -0.5),
        "exp_w_down": nrm(ks[22], (L, N_EXPERTS, EXPERT_DIM, D_MODEL), EXPERT_DIM ** -0.5),
        "sh_w_gate": nrm(ks[23], (L, D_MODEL, SHARED_DIM), D_MODEL ** -0.5),
        "sh_w_up": nrm(ks[24], (L, D_MODEL, SHARED_DIM), D_MODEL ** -0.5),
        "sh_w_down": nrm(ks[25], (L, SHARED_DIM, D_MODEL), SHARED_DIM ** -0.5),
    }

def reference(x, c, ctx, c_ctx, ada_w, ada_b, pre_mix_g, post_mix_g, pre_ffn_g, post_ffn_g,
              w_in, a_q_norm, a_k_norm, b_kv_norm, b_w_kv_up, c_sink, d_rpb, w_out,
              router_w, router_b, exp_w_gate, exp_w_up, exp_w_down, sh_w_gate, sh_w_up, sh_w_down):
    bsz, s_len, dm = x.shape
    cos_h, sin_h = _axial_rope(s_len, HEAD_DIM)
    cos_r, sin_r = _axial_rope(s_len, B_ROPE)
    xc = ctx
    c_act = jax.nn.silu(c)
    cc_act = jax.nn.silu(c_ctx)
    for l in range(DEPTH):
        with_ctx = l < DEPTH - 1
        mod = (c_act @ ada_w[l] + ada_b[l])[:, None, :]
        modc = cc_act @ ada_w[l] + ada_b[l]
        sh1, sc1, g1, sh2, sc2, g2 = jnp.split(mod, 6, axis=-1)
        sh1c, sc1c, g1c, sh2c, sc2c, g2c = jnp.split(modc, 6, axis=-1)

        h = _rms_norm(x, pre_mix_g[l]) * (1.0 + sc1) + sh1
        hc = _rms_norm(xc, pre_mix_g[l]) * (1.0 + sc1c) + sh1c
        p = _split_cols(h @ w_in[l])
        pc = _split_cols(hc @ w_in[l])
        oa, oa_c = _mixer_full_gqa(p[0], p[1], p[2], pc[0], pc[1], pc[2], a_q_norm[l], a_k_norm[l],
                                   cos_h, sin_h, with_ctx)
        ob, ob_c = _mixer_mla(p[3], p[4], p[5], pc[3], pc[4], pc[5], b_kv_norm[l], b_w_kv_up[l],
                              cos_r, sin_r, with_ctx)
        ow, ow_c = _mixer_window_gqa(p[6], p[7], p[8], pc[6], pc[7], pc[8], c_sink[l], cos_h, sin_h, with_ctx)
        on, on_c = _mixer_neighbourhood(p[9], p[10], p[11], pc[9], pc[10], pc[11], d_rpb[l], with_ctx)
        mix = jnp.concatenate([oa, ob, ow, on], axis=-1) @ w_out[l]
        x = x + g1 * _rms_norm(mix, post_mix_g[l])
        if with_ctx:
            mixc = jnp.concatenate([oa_c, ob_c, ow_c, on_c], axis=-1) @ w_out[l]
            xc = xc + g1c * _rms_norm(mixc, post_mix_g[l])

        h2 = (_rms_norm(x, pre_ffn_g[l]) * (1.0 + sc2) + sh2).reshape(-1, dm)
        if with_ctx:
            h2c = (_rms_norm(xc, pre_ffn_g[l]) * (1.0 + sc2c) + sh2c).reshape(-1, dm)
            tokens = jnp.concatenate([h2, h2c], axis=0)
        else:
            tokens = h2
        f = _moe(tokens, router_w[l], router_b[l], exp_w_gate[l], exp_w_up[l], exp_w_down[l],
                 sh_w_gate[l], sh_w_up[l], sh_w_down[l])
        n_lat = bsz * s_len
        x = x + g2 * _rms_norm(f[:n_lat].reshape(bsz, s_len, dm), post_ffn_g[l])
        if with_ctx:
            xc = xc + g2c * _rms_norm(f[n_lat:].reshape(bsz, -1, dm), post_ffn_g[l])
    return x


_drawn_inputs = setup_inputs


def setup_inputs(seed=0):
    import zlib

    import numpy as np

    out = dict(_drawn_inputs(seed))
    spreads = {}
    factors = {'a_q_norm': 2.885, 'a_k_norm': 2.699, 'c_sink': 8.0}
    for name, (base, spread) in spreads.items():
        noise = np.random.default_rng([zlib.crc32(name.encode()), seed]).standard_normal(out[name].shape)
        drawn = base * np.exp(spread * noise) if base else spread * noise
        out[name] = __import__('jax').numpy.asarray(drawn.astype(out[name].dtype))
    for name, factor in factors.items():
        out[name] = (out[name] * factor).astype(out[name].dtype)
    return out
```

```python
from contextlib import ExitStack

import numpy as np

import concourse.bass as bass
from concourse import mybir

F32 = mybir.dt.float32
F16 = mybir.dt.float16
I32 = mybir.dt.int32
U32 = mybir.dt.uint32
ALU = mybir.AluOpType
ACT = mybir.ActivationFunctionType
AX = mybir.AxisListType.X

P = 128
D = 1024
KD = D // P
DEPTH = 2
SEQ, CTX = 512, 256
LT, CT = SEQ // P, CTX // P
NT = LT + CT
HD = 64
GRID_W = 64
EPS = 1e-6
BIG = 3.0e38
NEG = -1e30
E = 64
NG, GE = 8, 8
TOPG = 4
FD = 256
ROUTED_SCALE = 2.5
NROW = NT * P
HROW = D + E
MAXB = (NROW * 8 + E * (P - 1)) // P + 1
TABN = P
U = 2
TIERS = (64, 96, 128)

GROUPS = (("A", 0, 512, 256, 0), ("B", 512, 544, 384, 256), ("C", 1056, 512, 256, 512), ("D", 1568, 768, 256, 768))
IN_W = 2336
SLOT_HEAD = (0, 2, 1, 3)

S_PRE, S_POST, S_PREF, S_POSTF, S_ADAB, S_KVG, S_SINK, S_GAIN, S_RB, S_W = 0, 8, 16, 24, 32, 80, 81, 85, 469, 533
C_ID, C_COS, C_SIN, C_COSR, C_SINR, C_PREV, C_NEXT, C_BAND, C_P, C_NEGP, C_TRASH, C_NEGB, C_THR, C_W = (
    0, 128, 384, 640, 768, 896, 1024, 1152, 1216, 1217, 1218, 1219, 1347, 1353)
H_TRI, H_ONE, H_IOTA, H_TIN, H_TST, H_TST128, H_TOK, H_W = 0, 128, 256, 384, 448, 512, 576, 588


class Signal:

    def __init__(self, sem):
        self.sem, self.base = sem, 0

    def wait(self, eng, count):
        if count > 0:
            eng.wait_ge(self.sem, self.base + count)

    def stage_over(self, total):
        self.base += total


def build(nc, t, stop=None):
    ctx = ExitStack()
    with ctx:
        signals = {}

        def S(name):
            if name not in signals:
                signals[name] = Signal(ctx.enter_context(nc.semaphore(name)))
            return signals[name]

        def sb(name, shape, dt=F32, scope=ctx):
            return scope.enter_context(nc.sbuf_tensor(name, shape, dt))

        ps = ctx.enter_context(nc.psum_tensor("ps", [P, 8, 512], F32))

        def banks(a, b):
            return ps[:, a:b, :].rearrange("p a n -> p (a n)")

        xs = sb("xs", [P, NT, D])
        cst = sb("cst", [P, C_W])
        csth = sb("csth", [P, H_W], F16)
        small = sb("small", [P, S_W])
        mods = sb("mods", [P, 8, 2, KD])
        csil = sb("csil", [P, KD, 2])
        half = sb("half", [P, 8])
        ident = cst[:, C_ID:C_ID + P]

        col_dram = nc.dram_tensor("col_scratch", (64, P), F32, kind="Internal").ap()
        h2_dram = nc.dram_tensor("h2_rows", (NROW + P, HROW), F32, kind="Internal").ap()
        acc_dram = nc.dram_tensor("ffn_rows", (NROW + P, D), F32, kind="Internal").ap()

        env = dict(nc=nc, t=t, S=S, sb=sb, ps=ps, banks=banks, xs=xs, cst=cst, csth=csth, small=small, mods=mods,
                   csil=csil, half=half, ident=ident, col_dram=col_dram, h2_dram=h2_dram, acc_dram=acc_dram)
        env = type("Env", (), env)
        load_all(env)
        for l in range(DEPTH):
            nt = NT if l < DEPTH - 1 else LT
            modulation(env, l, nt)
            with ExitStack() as mix:
                o_tok = sb(f"o_tok{l}", [P, nt, D], scope=mix)
                with ExitStack() as att:
                    hT = sb(f"hT{l}", [P, KD, NROW], scope=att)
                    wg = [sb(f"w_in{l}_{i}", [P, KD, 768], scope=att) for i in range(2)]
                    norm_in(env, l, hT, wg)
                    for g in range(4):
                        mixer(env, l, g, nt, hT, wg, o_tok)
                project_out(env, l, nt, o_tok)
            if stop == ("mix", l):
                break
            with ExitStack() as ffn:
                gm = sb(f"gm{l}", [P, nt, E], scope=ffn)
                table = sb(f"table{l}", [1, 2 * TABN + 2], I32, scope=ffn)
                route(env, l, nt, gm, table)
                if stop == ("route", l):
                    break
                experts(env, l, nt, gm, table)
            ffn_residual(env, l, nt)
            if stop == ("layer", l):
                break
        store(env)


def load_all(v):
    nc, S = v.nc, v.S
    loaded, silu, zero, zdone = S("start_loaded"), S("silu_done"), S("zeroed"), S("zeros_stored")
    with ExitStack() as scope:
        z = v.sb("zeros", [P, HROW], scope=scope)
        craw = v.sb("craw", [P, KD, 2], scope=scope)
        with nc.Block() as block:
            @block.sync
            def _(sp):
                sp.dma_start(craw[:, :, :], v.t["cvec"]).then_inc(loaded.sem, 16)
                sp.dma_start(v.cst[:, :], v.t["consts"]).then_inc(loaded.sem, 16)
                sp.dma_start(v.csth[:, :], v.t["consts16"]).then_inc(loaded.sem, 16)
                sp.dma_start(v.xs[:, 0:LT, :], v.t["x"].rearrange("(t p) d -> p t d", p=P)).then_inc(loaded.sem, 16)
                sp.dma_start(v.xs[:, LT:NT, :], v.t["ctx"].rearrange("(t p) d -> p t d", p=P)).then_inc(loaded.sem, 16)
                sp.wait_ge(loaded.sem, 80)

            @block.vector
            def _(dve):
                dve.memset(v.half[:, :], -0.5).then_inc(zero.sem, 1)
                dve.memset(z[:, :], 0.0).then_inc(zero.sem, 1)

            @block.gpsimd
            def _(pool):
                pool.wait_ge(zero.sem, 2)
                pool.dma_start(v.h2_dram[NROW:NROW + P, :], z[:, :]).then_inc(zdone.sem, 16)
                pool.wait_ge(zdone.sem, 16)

            @block.scalar
            def _(act):
                act.wait_ge(loaded.sem, 80)
                act.activation(v.csil[:, :, :], craw[:, :, :], ACT.Silu).then_inc(silu.sem, 1)
    silu.stage_over(1)


def modulation(v, l, nt):
    nc, S, small, mods = v.nc, v.S, v.small, v.mods
    nb, W = 12, 512
    s_small, s_w = S("small_loaded"), [S(f"ada_loaded{i}") for i in range(2)]
    s_mm, s_mod, s_t, s_te = S("mod_summed"), S("mod_columns"), S("mod_turned"), S("mod_turned_copied")
    s_cs = S("columns_stored")
    with ExitStack() as scope:
        aw = [v.sb(f"ada{l}_{i}", [P, KD, W], scope=scope) for i in range(2)]
        m = v.sb(f"modraw{l}", [P, 6, KD, 2], scope=scope)
        one_sc = v.sb(f"onesc{l}", [P, 2, KD, 2], scope=scope)
        turned = v.sb(f"turned{l}", [64, P], scope=scope)
        pm = v.banks(0, 1)[:, 0:96].rearrange("p (j c) -> p j c", c=2)
        pt = v.banks(1, 2)[0:64, 0:P]
        with nc.Block() as block:
            @block.sync
            def _(sp):
                sp.dma_start(small[:, :], v.t["small"][l]).then_inc(s_small.sem, 16)
                for b in range(nb):
                    s_mm.wait(sp, b - 1)
                    sp.dma_start(aw[b % 2][:, :, :], v.t["ada_w"][l, :, b * W:(b + 1) * W]
                                 .rearrange("(k p) n -> p k n", p=P)).then_inc(s_w[b % 2].sem, 16)
                s_te.wait(sp, 1)
                sp.dma_start(v.col_dram, turned[:, :]).then_inc(s_cs.sem, 16)
                s_cs.wait(sp, 16)

            @block.tensor
            def _(pe):
                for b in range(nb):
                    s_w[b % 2].wait(pe, 16 * (b // 2 + 1))
                    for j in range(W // P):
                        for k in range(KD):
                            last = pe.matmul(pm[:, b * 4 + j, :], aw[b % 2][:, k, j * P:(j + 1) * P], v.csil[:, k, :],
                                             start=(k == 0), stop=(k == KD - 1))
                    last.then_inc(s_mm.sem, 1)
                s_mod.wait(pe, 9)
                pe.transpose(pt, mods[:, 4:8, :, :].rearrange("p v c k -> p (v c k)"), v.ident).then_inc(s_t.sem, 1)

            @block.vector
            def _(dve):
                n = [0]

                def step(ins):
                    ins.then_inc(s_mod.sem, 1)
                    n[0] += 1
                    s_mod.wait(dve, n[0])

                s_small.wait(dve, 16)
                s_mm.wait(dve, nb)
                mv = m[:, :, :, :].rearrange("p s k c -> p (s k) c")
                adab = small[:, S_ADAB:S_ADAB + 48].unsqueeze(2).broadcast_to([P, 48, 2])
                step(dve.tensor_tensor(mv, pm, adab, ALU.add))
                step(dve.tensor_scalar(one_sc[:, 0, :, :], m[:, 1, :, :], 1.0, None, ALU.add))
                step(dve.tensor_scalar(one_sc[:, 1, :, :], m[:, 4, :, :], 1.0, None, ALU.add))

                def gain(c):
                    return small[:, c:c + KD].unsqueeze(1).broadcast_to([P, 2, KD])

                def ck(a):
                    return a.rearrange("p k c -> p c k")

                step(dve.tensor_tensor(mods[:, 0, :, :], ck(one_sc[:, 0, :, :]), gain(S_PRE), ALU.mult))
                step(dve.tensor_copy(mods[:, 1, :, :], ck(m[:, 0, :, :])))
                step(dve.tensor_tensor(mods[:, 4, :, :], ck(m[:, 2, :, :]), gain(S_POST), ALU.mult))
                step(dve.tensor_tensor(mods[:, 5, :, :], ck(one_sc[:, 1, :, :]), gain(S_PREF), ALU.mult))
                step(dve.tensor_copy(mods[:, 6, :, :], ck(m[:, 3, :, :])))
                step(dve.tensor_tensor(mods[:, 7, :, :], ck(m[:, 5, :, :]), gain(S_POSTF), ALU.mult))
                s_t.wait(dve, 1)
                dve.tensor_copy(turned[:, :], pt).then_inc(s_te.sem, 1)
    for s, k in ((s_small, 16), (s_w[0], 96), (s_w[1], 96), (s_mm, nb), (s_mod, 9), (s_t, 1), (s_te, 1), (s_cs, 16)):
        s.stage_over(k)


def norm_in(v, l, hT, wg):
    nc, S, mods = v.nc, v.S, v.mods
    s_sq, s_ms, s_rstd, s_xn, s_t, s_ea, s_ed = (S("squares"), S("mean_square"), S("rstd"), S("x_normed"), S("x_turned"),
                                                 S("turned_by_act"), S("turned_by_dve"))
    with ExitStack() as scope:
        junk = v.sb(f"junk{l}", [P, D], scope=scope)
        xn = v.sb(f"xn{l}", [P, 2, D], scope=scope)
        ss = v.sb(f"ss{l}", [P, 3, NT], scope=scope)
        pt = [v.ps[:, 0:2, :], v.ps[:, 2:4, :]]
        with nc.Block() as block:
            @block.sync
            def _(sp):
                load_w_in(v, sp, l, 0, wg)

            @block.scalar
            def _(act):
                def evac(i):
                    c = 0 if i < LT else 1
                    s_t.wait(act, i + 1)
                    for k in range(4):
                        last = act.activation(hT[:, k, i * P:(i + 1) * P], pt[i % 2][:, 0, k * P:(k + 1) * P], ACT.Identity,
                                              scale=mods[:, 0, c, k:k + 1], bias=mods[:, 1, c, k:k + 1])
                    last.then_inc(s_ea.sem, 1)

                for i in range(NT):
                    s_sq.wait(act, i)
                    act.activation(junk[:, :], v.xs[:, i, :], ACT.Square, accum_out=ss[:, 0, i:i + 1]).then_inc(s_sq.sem, 1)
                for i in range(NT):
                    s_rstd.wait(act, i + 1)
                    s_t.wait(act, i - 1)
                    act.activation(xn[:, i % 2, :], v.xs[:, i, :], ACT.Copy, scale=ss[:, 2, i:i + 1]).then_inc(s_xn.sem, 1)
                    if i:
                        evac(i - 1)
                evac(NT - 1)

            @block.vector
            def _(dve):
                for i in range(NT):
                    s_sq.wait(dve, i + 1)
                    dve.tensor_scalar(ss[:, 1, i:i + 1], ss[:, 0, i:i + 1], 1.0 / D, EPS, ALU.mult, ALU.add).then_inc(s_ms.sem, 1)
                for i in range(NT):
                    c = 0 if i < LT else 1
                    s_t.wait(dve, i + 1)
                    for k in range(4, 8):
                        last = dve.tensor_scalar(hT[:, k, i * P:(i + 1) * P], pt[i % 2][:, 1, (k - 4) * P:(k - 3) * P],
                                                 mods[:, 0, c, k:k + 1], mods[:, 1, c, k:k + 1], ALU.mult, ALU.add)
                    last.then_inc(s_ed.sem, 1)

            @block.gpsimd
            def _(pool):
                for i in range(NT):
                    s_ms.wait(pool, i + 1)
                    pool.tensor_tensor(ss[:, 2, i:i + 1], ss[:, 1, i:i + 1], v.half[:, 0:1], ALU.pow).then_inc(s_rstd.sem, 1)

            @block.tensor
            def _(pe):
                for i in range(NT):
                    s_xn.wait(pe, i + 1)
                    s_ea.wait(pe, i - 1)
                    s_ed.wait(pe, i - 1)
                    for k in range(KD):
                        last = pe.transpose(pt[i % 2][:, k // 4, (k % 4) * P:(k % 4 + 1) * P], xn[:, i % 2, k * P:(k + 1) * P], v.ident)
                    last.then_inc(s_t.sem, 1)
    for s in (s_sq, s_ms, s_rstd, s_xn, s_t, s_ea, s_ed):
        s.stage_over(NT)


def load_rows(v, eng, dst, vector, streams, signal):
    src = v.col_dram.rearrange("(v c k) p -> v c (k p)", v=4, c=2)[vector, 0:streams, :]
    eng.dma_start(dst, src.unsqueeze(0).broadcast_to([P, streams, D])).then_inc(signal.sem, 16)


def load_w_in(v, eng, l, g, wg):
    _, col, W, _, _ = GROUPS[g]
    eng.dma_start(wg[g % 2][:, :, 0:W], v.t["w_in"][l, :, col:col + W].rearrange("(k p) n -> p k n", p=P)
                  ).then_inc(v.S(f"w_in_loaded{g % 2}").sem, 16)


def mixer(v, l, g, nt, hT, wg, o_tok):
    nc, S, cst, small, ps = v.nc, v.S, v.cst, v.small, v.ps
    name, _, W, kv0, out0 = GROUPS[g]
    isA, isB, isC, isD = (name == x for x in "ABCD")
    KP = 96 if isB else P
    NQ, NK = (4, 4) if isB else (2, 2) if isD else (2, 1)
    qscale = float((HD + 32) ** -0.5) if isB else float(HD ** -0.5)
    has_q = [i < nt for i in range(NT)]
    nq = [sum(has_q[:i]) for i in range(NT + 1)]

    s_w = S(f"w_in_loaded{g % 2}")
    s_proj, s_v, s_rows, s_step = S("projected"), S("v_copied"), S("rows_ready"), S("dve_step")
    s_ms, s_rstd = S("head_mean_square"), S("head_rstd")
    s_t, s_qe, s_ke = S("qk_turned"), S("q_copied"), S("k_copied")
    s_cn, s_ct, s_ce, s_up, s_kn = S("latent_normed"), S("latent_turned"), S("latent_copied"), S("kv_up"), S("k_rows_copied")
    s_bias, s_band, s_wup = S("bias_loaded"), S("bias_masked"), S("w_kv_up_loaded")
    s_sc, s_max, s_exp, s_pt = S("scores"), S("negated_maximum"), S("exponentials"), S("probs_turned")
    s_pa, s_pd, s_pv, s_o, s_sx = S("probs_by_act"), S("probs_by_dve"), S("weighted_values"), S("out_written"), S("sink_exp")

    units = [(h, q) for h in range(4) for q in range(nt)]
    NU = len(units)

    def lo(u):
        q = units[u][1]
        if q >= LT:
            return 512
        if isC:
            return 512 - P * (min(q + 1, LT - 1) - max(q - 1, 0) + 1)
        return 0

    def key_tile(u, c):
        q = units[u][1]
        if c >= 4:
            return LT + c - 4
        return c - lo(u) // P + (max(q - 1, 0) if isC else 0)

    def head(slot):
        return SLOT_HEAD[slot] if isA or isC else slot

    def kv_of(slot):
        return slot % 2 if isA or isC else slot

    steps = []
    local = [sum(units[w][1] < LT for w in range(u + 1)) for u in range(NU)]

    with ExitStack() as scope:
        def sb(n, shape, dt=F32):
            return v.sb(f"{n}_{l}{name}", shape, dt, scope=scope)

        QT, KT, V = sb("QT", [P, NQ, NROW]), sb("KT", [P, NK, NROW]), sb("V", [P, NT, 256])
        R = sb("R", [P, 2, 768])
        T1, T2, T3, T4 = (sb(n, [P, 384]) for n in ("T1", "T2", "T3", "T4"))
        ss = sb("ss", [P, 3, NT, 8])
        if isB:
            wup = sb("wup", [P, 512])
            cn = sb("cn", [P, 2, P])
            cT = sb("cT", [P, 2, P])
        if isD:
            TD = sb("TD", [P, 4, 15, GRID_W])
        PR, PT = sb("PR", [P, 2, 768]), sb("PT", [P, 2, 768])
        st = sb("st", [P, 6, NU])

        pp = [v.banks(0, 2), v.banks(2, 4)]
        tq, tk = ps[:, 4, :], ps[:, 5, :]

        with nc.Block() as block:
            @block.sync
            def _(sp):
                if isB:
                    sp.dma_start(wup[:, :], v.t["w_up"][l]).then_inc(s_wup.sem, 16)
                if isD:
                    sp.dma_start(TD[:, :, :, :], v.t["bias"][l]).then_inc(s_bias.sem, 16)
                if g < 3:
                    load_w_in(v, sp, l, g + 1, wg)

            @block.gpsimd
            def _(pool):
                if isA or isB:
                    n = 6 if isA else 1
                    for i in range(NT):
                        a = 0 if has_q[i] or isB else 4
                        s_ms.wait(pool, i + 1)
                        pool.tensor_tensor(ss[:, 2, i, a:n], ss[:, 1, i, a:n], v.half[:, a:n], ALU.pow).then_inc(s_rstd.sem, 1)
                if isD:
                    s_bias.wait(pool, 16)
                    td = TD[:, :, :, :].rearrange("p h r c -> p (h r) c")
                    pool.tensor_tensor(td, td, cst[:, C_BAND:C_BAND + GRID_W].unsqueeze(1).broadcast_to([P, 60, GRID_W]),
                                       ALU.add).then_inc(s_band.sem, 1)

            @block.tensor
            def _(pe):
                def project(i):
                    s_rows.wait(pe, i - 1)
                    if not isB:
                        s_v.wait(pe, i - 1)
                    a = 0 if has_q[i] else kv0
                    for c0, c1 in ((a, min(W, 512)), (512, W)):
                        for k in range(KD if c1 > c0 else 0):
                            last = pe.matmul(pp[i % 2][:, c0:c1], hT[:, k, i * P:(i + 1) * P], wg[g % 2][:, k, c0:c1],
                                             start=(k == 0), stop=(k == KD - 1))
                    last.then_inc(s_proj.sem, 1)

                def latent(i):
                    s_cn.wait(pe, i + 1)
                    pe.transpose(ps[:, 7, 0:P], cn[:, i % 2, :], v.ident).then_inc(s_ct.sem, 1)
                    s_ce.wait(pe, i + 1)
                    s_kn.wait(pe, i)
                    pe.matmul(ps[:, 6, :], cT[:, i % 2, :], wup[:, :], start=True, stop=True).then_inc(s_up.sem, 1)

                def turn(i):
                    s_rows.wait(pe, i + 1)
                    if isB:
                        s_kn.wait(pe, i + 1)
                    s_qe.wait(pe, nq[i])
                    s_ke.wait(pe, i)
                    for j in range(0 if has_q[i] else NQ, NQ + NK):
                        dst, c = (tq, j) if j < NQ else (tk, j - NQ)
                        src = R[:, i % 2, j * KP:(j + 1) * KP]
                        last = pe.transpose(dst[0:KP, c * P:(c + 1) * P], src, v.ident)
                    last.then_inc(s_t.sem, 1)

                def scores(u):
                    s, q = units[u]
                    s_exp.wait(pe, u - 1)
                    if isB:
                        at, pair, kvp = 0, s, s
                    else:
                        at, pair, kvp = (s % 2) * HD, s // 2, s // 2 if isD else 0
                    rows = slice(at, at + (KP if isB else HD))
                    a, k0 = lo(u), key_tile(u, lo(u) // P) * P
                    lhs = QT[rows, pair, q * P:(q + 1) * P]
                    if a < 512:
                        pe.matmul(pp[u % 2][:, a:512], lhs, KT[rows, kvp, k0:k0 + 512 - a], start=True, stop=True)
                    pe.matmul(pp[u % 2][:, 512:768], lhs, KT[rows, kvp, SEQ:NROW], start=True, stop=True).then_inc(s_sc.sem, 1)

                def turn_probs(u):
                    s_exp.wait(pe, u + 1)
                    s_o.wait(pe, u - 1)
                    b = 4 + 2 * (u % 2)
                    for c in range(lo(u) // P, 6):
                        last = pe.transpose(ps[:, b + c // 4, (c % 4) * P:(c % 4 + 1) * P], PR[:, u % 2, c * P:(c + 1) * P], v.ident)
                    last.then_inc(s_pt.sem, 1)

                def values(u):
                    s_pa.wait(pe, local[u])
                    s_pd.wait(pe, u + 1)
                    c0 = kv_of(units[u][0]) * HD
                    for c in range(lo(u) // P, 6):
                        last = pe.matmul(ps[:, 5 + 2 * (u % 2), 256:256 + HD], PT[:, u % 2, c * P:(c + 1) * P],
                                         V[:, key_tile(u, c), c0:c0 + HD], start=(c == lo(u) // P), stop=(c == 5))
                    last.then_inc(s_pv.sem, 1)

                s_w.wait(pe, 16)
                if isB:
                    s_wup.wait(pe, 16)
                project(0)
                for i in range(NT):
                    if i + 1 < NT:
                        project(i + 1)
                    if isB:
                        latent(i)
                    turn(i)
                s_qe.wait(pe, nq[NT])
                s_ke.wait(pe, NT)
                if not isB:
                    s_v.wait(pe, NT)
                scores(0)
                for u in range(NU):
                    if u + 1 < NU:
                        scores(u + 1)
                    if u:
                        values(u - 1)
                    turn_probs(u)
                values(NU - 1)

            @block.scalar
            def _(act):
                for i in range(NT):
                    tok = slice(i * P, (i + 1) * P)
                    a = 0 if has_q[i] else kv0
                    if isA or isC:
                        s_proj.wait(act, i + 1)
                        act.copy(V[:, i, 0:P], pp[i % 2][:, 384:512]).then_inc(s_v.sem, 1)
                    if isD:
                        s_proj.wait(act, i + 1)
                        s_t.wait(act, i - 1)
                        act.copy(R[:, i % 2, a:512], pp[i % 2][:, a:512]).then_inc(s_rows.sem, 1)
                    if isB:
                        s_ct.wait(act, i + 1)
                        act.activation(cT[:, i % 2, :], ps[:, 7, 0:P], ACT.Copy, scale=small[:, S_KVG:S_KVG + 1]).then_inc(s_ce.sem, 1)
                        s_up.wait(act, i + 1)
                        s_t.wait(act, i - 1)
                        up = ps[:, 6, :].rearrange("p (h c) -> p h c", h=4)
                        act.copy(V[:, i, :].rearrange("p (h c) -> p h c", h=4), up[:, :, HD:])
                        act.copy(R[:, i % 2, :].rearrange("p (h c) -> p h c", h=8)[:, 4:8, 0:HD], up[:, :, 0:HD]).then_inc(s_kn.sem, 1)
                    if has_q[i]:
                        s_t.wait(act, i + 1)
                        act.mul(QT[0:KP, :, tok], tq[0:KP, 0:NQ * P].rearrange("p (j c) -> p j c", j=NQ), qscale).then_inc(s_qe.sem, 1)

                def exps(u):
                    s_max.wait(act, u + 1)
                    s_pt.wait(act, u - 1)
                    a = lo(u)
                    if isC:
                        act.activation(st[:, 3, u:u + 1], small[:, S_SINK + units[u][0]:S_SINK + units[u][0] + 1], ACT.Exp,
                                       bias=st[:, 1, u:u + 1])
                    act.activation(PR[:, u % 2, a:768], pp[u % 2][:, a:768], ACT.Exp, bias=st[:, 1, u:u + 1],
                                   accum_out=st[:, 2, u:u + 1]).then_inc(s_exp.sem, 1)

                exps(0)
                for u in range(NU):
                    if u + 1 < NU:
                        exps(u + 1)
                    if lo(u) < 512:
                        s_pt.wait(act, u + 1)
                        s_pv.wait(act, u - 1)
                        act.copy(PT[:, u % 2, lo(u):512], ps[:, 4 + 2 * (u % 2), lo(u):512]).then_inc(s_pa.sem, 1)

            @block.vector
            def _(dve):
                n = [0]

                def step(ins):
                    ins.then_inc(s_step.sem, 1)
                    n[0] += 1
                    s_step.wait(dve, n[0])

                def heads(ap, w=HD):
                    return ap.rearrange("p (h c) -> p h c", c=w)

                def rope(dst, src, nh, w, cos, sin, i):
                    c = cst[:, cos + i * w:cos + (i + 1) * w].unsqueeze(1).broadcast_to([P, nh, w])
                    sn = cst[:, sin + i * w:sin + (i + 1) * w].rearrange("p (a b c) -> p a b c", a=2, b=2)
                    t2 = T2[:, 0:nh * w].rearrange("p (h a b c) -> p h a b c", h=nh, a=2, b=2)
                    s4 = src.rearrange("p h (a b c) -> p h a b c", a=2, b=2)
                    for b in range(2):
                        dve.tensor_tensor(t2[:, :, :, b, :], s4[:, :, :, 1 - b, :],
                                          sn[:, :, b, :].unsqueeze(1).broadcast_to([P, nh, 2, w // 4]), ALU.mult)
                    t3 = heads(T3[:, 0:nh * w], w)
                    step(dve.tensor_tensor(t3, src, c, ALU.mult))
                    return dve.tensor_tensor(dst, t3, heads(T2[:, 0:nh * w], w), ALU.add)

                for i in range(NT):
                    tok = slice(i * P, (i + 1) * P)
                    pr = pp[i % 2]
                    s_proj.wait(dve, i + 1)
                    if isA or isC:
                        s_v.wait(dve, i + 1)
                        a = 0 if has_q[i] else 256
                        nh = (384 - a) // HD
                        src = heads(pr[:, a:384])
                        dst = heads(R[:, i % 2, a:384])
                        s_t.wait(dve, i - 1)
                    if isA:
                        h0 = a // HD
                        t1, raw = heads(T1[:, 0:nh * HD]), heads(T4[:, 0:nh * HD])
                        step(dve.tensor_copy(raw, src))
                        step(dve.tensor_tensor(t1, raw, raw, ALU.mult))
                        step(dve.tensor_reduce(ss[:, 0, i, h0:6], t1, AX, ALU.add))
                        dve.tensor_scalar(ss[:, 1, i, h0:6], ss[:, 0, i, h0:6], 1.0 / HD, EPS, ALU.mult, ALU.add).then_inc(s_ms.sem, 1)
                        s_rstd.wait(dve, i + 1)
                        step(dve.tensor_tensor(t1, raw, ss[:, 2, i, h0:6].unsqueeze(2).broadcast_to([P, nh, HD]), ALU.mult))
                        gain = heads(small[:, S_GAIN + a:S_GAIN + 384])
                        if i < LT:
                            step(dve.tensor_tensor(t1, t1, gain, ALU.mult))
                            rope(dst, t1, nh, HD, C_COS, C_SIN, i).then_inc(s_rows.sem, 1)
                        else:
                            dve.tensor_tensor(dst, t1, gain, ALU.mult).then_inc(s_rows.sem, 1)
                    elif isC:
                        if i < LT:
                            rope(dst, src, nh, HD, C_COS, C_SIN, i).then_inc(s_rows.sem, 1)
                        else:
                            dve.tensor_copy(dst, src).then_inc(s_rows.sem, 1)
                    elif isD:
                        dve.tensor_copy(V[:, i, :], pr[:, 512:768]).then_inc(s_v.sem, 1)
                    elif isB:
                        s_t.wait(dve, i - 1)
                        r8 = heads(R[:, i % 2, :], 96)
                        lat = pr[:, 384:512]
                        step(dve.tensor_copy(T4[:, 0:P], lat))
                        step(dve.tensor_tensor(T1[:, 0:P], T4[:, 0:P], T4[:, 0:P], ALU.mult))
                        step(dve.tensor_reduce(ss[:, 0, i, 0:1], T1[:, 0:P], AX, ALU.add))
                        dve.tensor_scalar(ss[:, 1, i, 0:1], ss[:, 0, i, 0:1], 1.0 / P, EPS, ALU.mult, ALU.add).then_inc(s_ms.sem, 1)
                        s_rstd.wait(dve, i + 1)
                        s_ct.wait(dve, i - 1)
                        dve.tensor_scalar(cn[:, i % 2, :], T4[:, 0:P], ss[:, 2, i, 0:1], None, ALU.mult).then_inc(s_cn.sem, 1)
                        q4 = heads(pr[:, 0:384], 96)
                        kr = pr[:, 512:544].unsqueeze(1)
                        if i < LT:
                            step(dve.tensor_copy(r8[:, 0:4, 0:HD], q4[:, :, 0:HD]))
                            step(rope(r8[:, 0:4, HD:], q4[:, :, HD:], 4, 32, C_COSR, C_SINR, i))
                            k1 = T1[:, 256:288].unsqueeze(1)
                            step(rope(k1, kr, 1, 32, C_COSR, C_SINR, i))
                            dve.tensor_copy(r8[:, 4:8, HD:], k1.broadcast_to([P, 4, 32])).then_inc(s_rows.sem, 1)
                        else:
                            if has_q[i]:
                                step(dve.tensor_copy(r8[:, 0:4, :], q4))
                            dve.tensor_copy(r8[:, 4:8, HD:], kr.broadcast_to([P, 4, 32])).then_inc(s_rows.sem, 1)
                    s_t.wait(dve, i + 1)
                    dve.tensor_copy(KT[0:KP, :, tok], tk[0:KP, 0:NK * P].rearrange("p (j c) -> p j c", j=NK)).then_inc(s_ke.sem, 1)

                def maximum(u):
                    s, q = units[u]
                    s_sc.wait(dve, u + 1)
                    sc = pp[u % 2]
                    if isD and q < LT:
                        if u == 0:
                            s_band.wait(dve, 1)
                        b = TD[:, s, 7 - 2 * q:15 - 2 * q, :].rearrange("p r c -> p (r c)")
                        step(dve.tensor_tensor(sc[:, 0:512], sc[:, 0:512], b, ALU.add))
                    if isC and 0 < q < LT:
                        a = lo(u)
                        step(dve.tensor_tensor(sc[:, a:a + P], sc[:, a:a + P], cst[:, C_PREV:C_PREV + P], ALU.add))
                    if isC and q < LT - 1:
                        step(dve.tensor_tensor(sc[:, 384:512], sc[:, 384:512], cst[:, C_NEXT:C_NEXT + P], ALU.add))
                    step(dve.tensor_reduce(st[:, 0, u:u + 1], sc[:, lo(u):768], AX, ALU.max))
                    if isC:
                        ins = dve.tensor_scalar(st[:, 1, u:u + 1], st[:, 0, u:u + 1], small[:, S_SINK + s:S_SINK + s + 1], -1.0,
                                                ALU.max, ALU.mult)
                    else:
                        ins = dve.tensor_scalar(st[:, 1, u:u + 1], st[:, 0, u:u + 1], -1.0, None, ALU.mult)
                    ins.then_inc(s_max.sem, 1)

                def divide(u):
                    s, q = units[u]
                    s_pv.wait(dve, u + 1)
                    den = st[:, 2, u:u + 1]
                    if isC:
                        step(dve.tensor_tensor(st[:, 4, u:u + 1], den, st[:, 3, u:u + 1], ALU.add))
                        den = st[:, 4, u:u + 1]
                    step(dve.reciprocal(st[:, 5, u:u + 1], den))
                    c = out0 + head(s) * HD
                    dve.tensor_scalar(o_tok[:, q, c:c + HD], ps[:, 5 + 2 * (u % 2), 256:256 + HD], st[:, 5, u:u + 1], None,
                                      ALU.mult).then_inc(s_o.sem, 1)

                maximum(0)
                for u in range(NU):
                    if u + 1 < NU:
                        maximum(u + 1)
                    if u:
                        divide(u - 1)
                    s_pt.wait(dve, u + 1)
                    s_pv.wait(dve, u - 1)
                    dve.tensor_copy(PT[:, u % 2, 512:768], ps[:, 5 + 2 * (u % 2), 0:256]).then_inc(s_pd.sem, 1)
                divide(NU - 1)
                steps.append(n[0])

    steps_total = steps.pop()
    s_w.stage_over(16)
    for s, k in ((s_proj, NT), (s_rows, NT), (s_t, NT), (s_qe, nq[NT]), (s_ke, NT), (s_step, steps_total),
                 (s_sc, NU), (s_max, NU), (s_exp, NU), (s_pt, NU), (s_pa, local[-1]), (s_pd, NU), (s_pv, NU), (s_o, NU)):
        s.stage_over(k)
    if not isB:
        s_v.stage_over(NT)
    if isA or isB:
        s_ms.stage_over(NT)
        s_rstd.stage_over(NT)
    if isB:
        for s, k in ((s_cn, NT), (s_ct, NT), (s_ce, NT), (s_up, NT), (s_kn, NT), (s_wup, 16)):
            s.stage_over(k)
    if isD:
        s_bias.stage_over(16)
        s_band.stage_over(1)


def stepper(dve, signal, counts):
    counts.append(0)

    def step(ins):
        ins.then_inc(signal.sem, 1)
        counts[-1] += 1
        signal.wait(dve, counts[-1])
    return step


def project_out(v, l, nt, o_tok):
    nc, S, ps = v.nc, v.S, v.ps
    streams = 2 if nt == NT else 1
    s_w, s_row, s_t, s_ea, s_ed = S("w_out_loaded"), S("gate_row_loaded"), S("out_turned"), S("turned_by_act"), S("turned_by_dve")
    s_mm, s_sq, s_ms, s_rstd, s_x, s_step = S("mixed"), S("squares"), S("mean_square"), S("rstd"), S("x_updated"), S("dve_step")
    counts = []
    with ExitStack() as scope:
        w = v.sb(f"w_out{l}", [P, KD, D], scope=scope)
        g1 = v.sb(f"g1_{l}", [P, streams, D], scope=scope)
        oT = v.sb(f"oT{l}", [P, 2, KD, P], scope=scope)
        junk = v.sb(f"mjunk{l}", [P, D], scope=scope)
        add = v.sb(f"madd{l}", [P, D], scope=scope)
        ss = v.sb(f"mss{l}", [P, 3, NT], scope=scope)
        with nc.Block() as block:
            @block.sync
            def _(sp):
                src = v.t["w_out"][l].rearrange("(k p) n -> p k n", p=P)
                for k in range(0, KD, 2):
                    sp.dma_start(w[:, k:k + 2, :], src[:, k:k + 2, :]).then_inc(s_w.sem, 16)
                load_rows(v, sp, g1[:, :, :], 0, streams, s_row)

            @block.tensor
            def _(pe):
                def turn(i):
                    s_ea.wait(pe, i - 1)
                    s_ed.wait(pe, i - 1)
                    for k in range(KD):
                        last = pe.transpose(ps[:, 4 + 2 * (i % 2) + k // 4, (k % 4) * P:(k % 4 + 1) * P], o_tok[:, i, k * P:(k + 1) * P], v.ident)
                    last.then_inc(s_t.sem, 1)

                turn(0)
                for i in range(nt):
                    if i + 1 < nt:
                        turn(i + 1)
                    s_ea.wait(pe, i + 1)
                    s_ed.wait(pe, i + 1)
                    s_x.wait(pe, i - 1)
                    if i == 0:
                        s_w.wait(pe, 64)
                    for n in range(2):
                        for k in range(KD):
                            last = pe.matmul(ps[:, 2 * (i % 2) + n, :], oT[:, i % 2, k, :], w[:, k, n * 512:(n + 1) * 512],
                                             start=(k == 0), stop=(k == KD - 1))
                    last.then_inc(s_mm.sem, 1)

            @block.scalar
            def _(act):
                def evac(i):
                    s_t.wait(act, i + 1)
                    s_mm.wait(act, i - 1)
                    act.copy(oT[:, i % 2, 0:4, :].rearrange("p k c -> p (k c)"), ps[:, 4 + 2 * (i % 2), :]).then_inc(s_ea.sem, 1)

                evac(0)
                for i in range(nt):
                    if i + 1 < nt:
                        evac(i + 1)
                    s_mm.wait(act, i + 1)
                    s_sq.wait(act, i)
                    act.activation(junk[:, :], v.banks(2 * (i % 2), 2 * (i % 2) + 2), ACT.Square,
                                   accum_out=ss[:, 0, i:i + 1]).then_inc(s_sq.sem, 1)

            @block.gpsimd
            def _(pool):
                for i in range(nt):
                    s_ms.wait(pool, i + 1)
                    pool.tensor_tensor(ss[:, 2, i:i + 1], ss[:, 1, i:i + 1], v.half[:, 0:1], ALU.pow).then_inc(s_rstd.sem, 1)

            @block.vector
            def _(dve):
                step = stepper(dve, s_step, counts)

                def evac(i):
                    s_t.wait(dve, i + 1)
                    s_mm.wait(dve, i - 1)
                    dve.tensor_copy(oT[:, i % 2, 4:8, :].rearrange("p k c -> p (k c)"), ps[:, 5 + 2 * (i % 2), :]).then_inc(s_ed.sem, 1)

                s_row.wait(dve, 16)
                evac(0)
                for i in range(nt):
                    if i + 1 < nt:
                        evac(i + 1)
                    s_sq.wait(dve, i + 1)
                    dve.tensor_scalar(ss[:, 1, i:i + 1], ss[:, 0, i:i + 1], 1.0 / D, EPS, ALU.mult, ALU.add).then_inc(s_ms.sem, 1)
                    s_rstd.wait(dve, i + 1)
                    s_x.wait(dve, i)
                    step(dve.scalar_tensor_tensor(out=add[:, :], in0=v.banks(2 * (i % 2), 2 * (i % 2) + 2), scalar=ss[:, 2, i:i + 1],
                                                  in1=g1[:, 0 if i < LT else 1, :], op0=ALU.mult, op1=ALU.mult))
                    dve.tensor_tensor(v.xs[:, i, :], v.xs[:, i, :], add[:, :], ALU.add).then_inc(s_x.sem, 1)
    for s, k in ((s_w, 64), (s_row, 16), (s_t, nt), (s_ea, nt), (s_ed, nt), (s_mm, nt), (s_sq, nt), (s_ms, nt), (s_rstd, nt),
                 (s_x, nt), (s_step, counts[0])):
        s.stage_over(k)


def route(v, l, nt, gm, table):
    nc, S, ps, small, csth = v.nc, v.S, v.ps, v.small, v.csth
    streams = 2 if nt == NT else 1
    NTOK = nt * P
    pieces = [(0, 512)] + ([(512, 768)] if nt == NT else [])
    work = [(f, a, b) for a, b in pieces for f in range(2)]
    s_row, s_rw, s_sw = S("ffn_rows_loaded"), S("router_loaded"), S("shared_loaded")
    s_sq, s_ms, s_rstd, s_h = S("squares"), S("mean_square"), S("rstd"), S("h2_ready")
    s_st = [S("h2_stored0"), S("h2_stored1")]
    s_t, s_ea, s_ed, s_step = S("h2_turned"), S("turned_by_act"), S("turned_by_dve"), S("dve_step")
    s_lg, s_ex, s_wt, s_ws = S("logits"), S("logits_exp"), S("weights_ready"), S("weights_stored")
    s_gu, s_si, s_g = S("shared_gate_up"), S("shared_silu"), S("shared_hidden")
    s_dn, s_ya, s_yd = S("shared_down"), S("shared_by_act"), S("shared_by_dve")
    s_ys = [S("shared_stored0"), S("shared_stored1")]
    s_sel, s_cnt, s_nb, s_slot, s_tab, s_tt = S("chosen"), S("counted"), S("blocks_counted"), S("slots"), S("table_columns"), S("table_turned")
    counts = []
    with ExitStack() as scope:
        def sb(n, shape, dt=F32):
            return v.sb(f"{n}_{l}", shape, dt, scope=scope)

        ab = sb("ab", [P, 2, streams, D])
        rw = sb("rw", [P, KD, E])
        sgu = sb("sgu", [P, KD, 2, FD])
        sd = sb("sd", [P, 2, D])
        H = sb("H", [P, 2, D])
        hT = sb("h2T", [P, KD, NTOK])
        junk = sb("rjunk", [P, D])
        ss = sb("rss", [P, 3, NT])
        SGx = sb("SGx", [P, 2, 512])
        G = sb("G", [P, 2, NTOK])
        Y = sb("Ysh", [P, 2, D])
        ex, sc, sbv, cand, mr, w = (sb(n, [P, nt, E]) for n in ("ex", "sc", "sbv", "cand", "mr", "wts"))
        sel = sb("sel", [P, nt, E], F16)
        g8, m8, rp, i12, o12 = sb("g8", [P, nt, NG, 8]), sb("m8", [P, nt, 8]), sb("rp", [P, nt, 8]), sb("i12", [P, nt, 12]), sb("o12", [P, nt, 12])
        gk, pen, wsum = sb("gk", [P, nt, NG]), sb("pen", [P, nt, NG]), sb("wsum", [P, 2, nt])
        cc = sb("cc", [E, 8])
        nbb = sb("nbb", [E, P], F16)
        cnt, cst128, o1, o2 = (sb(n, [P, E]) for n in ("cnt", "cst128", "o1", "o2"))
        tb = sb("tb", [P, 6])

        with nc.Block() as block:
            @block.sync
            def _(sp):
                for r in range(2):
                    load_rows(v, sp, ab[:, r, :, :], 1 + r, streams, s_row)
                sp.dma_start(rw[:, :, :], v.t["router_w"][l].rearrange("(k p) n -> p k n", p=P)).then_inc(s_rw.sem, 16)
                sp.dma_start(sgu[:, :, 0, :], v.t["sh_g"][l].rearrange("(k p) n -> p k n", p=P)).then_inc(s_sw.sem, 16)
                sp.dma_start(sgu[:, :, 1, :], v.t["sh_u"][l].rearrange("(k p) n -> p k n", p=P)).then_inc(s_sw.sem, 16)
                sp.dma_start(sd[:, :, :], v.t["sh_d"][l].rearrange("(f p) n -> p f n", p=P)).then_inc(s_sw.sem, 16)
                for i in range(nt):
                    s_h.wait(sp, i + 1)
                    sp.dma_start(v.h2_dram[i * P:(i + 1) * P, 0:D], H[:, i % 2, :]).then_inc(s_st[i % 2].sem, 16)
                s_wt.wait(sp, 1)
                sp.dma_start(v.h2_dram[0:NTOK, D:HROW].rearrange("(t p) e -> p t e", p=P), w[:, :, :]).then_inc(s_ws.sem, 16)
                for i in range(nt):
                    s_ya.wait(sp, i + 1)
                    s_yd.wait(sp, i + 1)
                    sp.dma_start(v.acc_dram[i * P:(i + 1) * P, :], Y[:, i % 2, :]).then_inc(s_ys[i % 2].sem, 16)
                for j in range(2):
                    s_st[j].wait(sp, 16 * (nt // 2))
                    s_ys[j].wait(sp, 16 * (nt // 2))
                s_ws.wait(sp, 16)

            @block.gpsimd
            def _(pool):
                for i in range(nt):
                    s_ms.wait(pool, i + 1)
                    pool.tensor_tensor(ss[:, 2, i:i + 1], ss[:, 1, i:i + 1], v.half[:, 0:1], ALU.pow).then_inc(s_rstd.sem, 1)

            @block.tensor
            def _(pe):
                for i in range(nt):
                    s_h.wait(pe, i + 1)
                    s_ea.wait(pe, i - 1)
                    s_ed.wait(pe, i - 1)
                    for k in range(KD):
                        last = pe.transpose(ps[:, 4 + 2 * (i % 2) + k // 4, (k % 4) * P:(k % 4 + 1) * P], H[:, i % 2, k * P:(k + 1) * P], v.ident)
                    last.then_inc(s_t.sem, 1)
                s_ea.wait(pe, nt)
                s_ed.wait(pe, nt)
                s_rw.wait(pe, 16)
                for i in range(nt):
                    for k in range(KD):
                        last = pe.matmul(ps[:, 0, i * E:(i + 1) * E], hT[:, k, i * P:(i + 1) * P], rw[:, k, :], start=(k == 0), stop=(k == KD - 1))
                last.then_inc(s_lg.sem, 1)
                s_sw.wait(pe, 48)
                for n, (f, a, b) in enumerate(work):
                    s_g.wait(pe, n - 2)
                    for h in range(2):
                        for k in range(KD):
                            last = pe.matmul(ps[:, 1 + 2 * (n % 3) + h, 0:b - a], sgu[:, k, h, f * P:(f + 1) * P], hT[:, k, a:b],
                                             start=(k == 0), stop=(k == KD - 1))
                    last.then_inc(s_gu.sem, 1)
                s_ex.wait(pe, 1)
                s_sel.wait(pe, 1)
                ones = csth[:, H_ONE:H_ONE + P]
                for i in range(nt):
                    pe.matmul(ps[:, 0, 0:E], ones, sel[:, i, :], start=(i == 0), stop=(i == nt - 1))
                for i in range(nt):
                    last = pe.matmul(ps[0:E, 0, E:E + 1], sel[:, i, :], ones[:, 0:1], start=(i == 0), stop=(i == nt - 1))
                last.then_inc(s_cnt.sem, 1)

                def down(i):
                    s_g.wait(pe, len(work))
                    s_ya.wait(pe, i - 1)
                    s_yd.wait(pe, i - 1)
                    for n in range(2):
                        for f in range(2):
                            last = pe.matmul(ps[:, 1 + 2 * (i % 2) + n, :], G[:, f, i * P:(i + 1) * P], sd[:, f, n * 512:(n + 1) * 512],
                                             start=(f == 0), stop=(f == 1))
                    last.then_inc(s_dn.sem, 1)

                down(0)
                down(1)
                s_nb.wait(pe, 1)
                pe.matmul(ps[:, 0, 0:E], nbb[:, :], csth[0:E, H_TIN:H_TIN + E], start=True, stop=True)
                pe.matmul(ps[:, 0, E:2 * E], nbb[:, :], csth[0:E, H_TST:H_TST + E], start=True, stop=True)
                for i in range(nt):
                    out = ps[:, 7, i * E:(i + 1) * E]
                    pe.matmul(out, nbb[:, :], csth[0:E, H_TST128:H_TST128 + E], start=True, stop=False)
                    for j in range(i):
                        pe.matmul(out, ones, sel[:, j, :], start=False, stop=False)
                    last = pe.matmul(out, csth[:, H_TRI:H_TRI + P], sel[:, i, :], start=False, stop=True)
                last.then_inc(s_slot.sem, 1)
                down(2)
                down(3)
                s_tab.wait(pe, 1)
                for c in range(2):
                    last = pe.matmul(ps[0:1, 0, c * P:(c + 1) * P], tb[:, 4 + c:5 + c], v.ident, start=True, stop=True)
                last.then_inc(s_tt.sem, 1)
                for i in range(4, nt):
                    down(i)

            @block.scalar
            def _(act):
                for i in range(nt):
                    s_sq.wait(act, i)
                    act.activation(junk[:, :], v.xs[:, i, :], ACT.Square, accum_out=ss[:, 0, i:i + 1]).then_inc(s_sq.sem, 1)
                for i in range(nt):
                    s_t.wait(act, i + 1)
                    act.copy(hT[:, 0:4, i * P:(i + 1) * P], ps[:, 4 + 2 * (i % 2), :].rearrange("p (k c) -> p k c", k=4)).then_inc(s_ea.sem, 1)
                s_lg.wait(act, 1)
                act.activation(ex[:, :, :].rearrange("p t e -> p (t e)"), ps[:, 0, 0:nt * E], ACT.Exp, scale=-1.0).then_inc(s_ex.sem, 1)
                for n, (f, a, b) in enumerate(work):
                    s_gu.wait(act, n + 1)
                    s_g.wait(act, n - 1)
                    act.activation(SGx[:, n % 2, 0:b - a], ps[:, 1 + 2 * (n % 3), 0:b - a], ACT.Silu).then_inc(s_si.sem, 1)
                for i in range(nt):
                    s_dn.wait(act, i + 1)
                    s_ys[i % 2].wait(act, 16 * (i // 2))
                    act.copy(Y[:, i % 2, 0:512], ps[:, 1 + 2 * (i % 2), :]).then_inc(s_ya.sem, 1)

            @block.vector
            def _(dve):
                step = stepper(dve, s_step, counts)
                for i in range(nt):
                    s_sq.wait(dve, i + 1)
                    dve.tensor_scalar(ss[:, 1, i:i + 1], ss[:, 0, i:i + 1], 1.0 / D, EPS, ALU.mult, ALU.add).then_inc(s_ms.sem, 1)
                s_row.wait(dve, 32)

                def h2(i):
                    c = 0 if i < LT else 1
                    s_rstd.wait(dve, i + 1)
                    s_t.wait(dve, i - 1)
                    s_st[i % 2].wait(dve, 16 * (i // 2))
                    step(dve.scalar_tensor_tensor(out=H[:, i % 2, :], in0=v.xs[:, i, :], scalar=ss[:, 2, i:i + 1], in1=ab[:, 0, c, :],
                                                  op0=ALU.mult, op1=ALU.mult))
                    dve.tensor_tensor(H[:, i % 2, :], H[:, i % 2, :], ab[:, 1, c, :], ALU.add).then_inc(s_h.sem, 1)

                h2(0)
                for i in range(nt):
                    if i + 1 < nt:
                        h2(i + 1)
                    s_t.wait(dve, i + 1)
                    dve.tensor_copy(hT[:, 4:8, i * P:(i + 1) * P], ps[:, 5 + 2 * (i % 2), :].rearrange("p (k c) -> p k c", k=4)).then_inc(s_ed.sem, 1)
                s_ex.wait(dve, 1)
                rb = small[:, S_RB:S_RB + E].unsqueeze(1).broadcast_to([P, nt, E])
                step(dve.tensor_scalar(ex[:, :, :], ex[:, :, :], 1.0, None, ALU.add))
                step(dve.reciprocal(sc[:, :, :], ex[:, :, :]))
                step(dve.tensor_tensor(sbv[:, :, :], sc[:, :, :], rb, ALU.add))
                for i in range(nt):
                    for g in range(NG):
                        dve.max(g8[:, i, g, :], sbv[:, i, g * GE:(g + 1) * GE])
                dve.memset(i12[:, :, 8:12], -BIG)
                step(dve.memset(rp[:, :, TOPG:8], -BIG))
                step(dve.tensor_tensor(i12[:, :, 0:8], g8[:, :, :, 0], g8[:, :, :, 1], ALU.add))
                for i in range(nt):
                    last = dve.max(m8[:, i, :], i12[:, i, 0:8])
                step(last)
                step(dve.tensor_copy(rp[:, :, 0:TOPG], m8[:, :, 0:TOPG]))
                for i in range(nt):
                    last = dve.match_replace(o12[:, i, :], rp[:, i, :], i12[:, i, :], BIG)
                step(last)
                step(dve.tensor_scalar(gk[:, :, :], o12[:, :, 0:8], BIG, None, ALU.is_equal))
                step(dve.tensor_scalar(pen[:, :, :], gk[:, :, :], -1.0, BIG, ALU.add, ALU.mult))

                def by_group(a):
                    return a.rearrange("p t (g e) -> p (t g) e", g=NG)

                def over_group(a):
                    return a.rearrange("p t g -> p (t g)").unsqueeze(2).broadcast_to([P, nt * NG, GE])

                step(dve.tensor_tensor(by_group(cand[:, :, :]), by_group(sbv[:, :, :]), over_group(gk[:, :, :]), ALU.mult))
                step(dve.tensor_tensor(by_group(cand[:, :, :]), by_group(cand[:, :, :]), over_group(pen[:, :, :]), ALU.add))
                for i in range(nt):
                    last = dve.max(m8[:, i, :], cand[:, i, :])
                step(last)
                for i in range(nt):
                    last = dve.match_replace(mr[:, i, :], m8[:, i, :], cand[:, i, :], BIG)
                step(last)
                dve.tensor_scalar(sel[:, :, :], mr[:, :, :], BIG, None, ALU.is_equal).then_inc(s_sel.sem, 1)
                step(dve.tensor_scalar(mr[:, :, :], mr[:, :, :], BIG, None, ALU.is_equal))
                step(dve.tensor_tensor(w[:, :, :], sc[:, :, :], mr[:, :, :], ALU.mult))
                step(dve.tensor_reduce(wsum[:, 0, :], w[:, :, :], AX, ALU.add))
                step(dve.reciprocal(wsum[:, 1, :], wsum[:, 0, :]))
                dve.scalar_tensor_tensor(out=w[:, :, :], in0=w[:, :, :], scalar=ROUTED_SCALE, in1=wsum[:, 1, :].unsqueeze(2).broadcast_to([P, nt, E]),
                                         op0=ALU.mult, op1=ALU.mult).then_inc(s_wt.sem, 1)
                for n, (f, a, b) in enumerate(work):
                    s_si.wait(dve, n + 1)
                    dve.tensor_tensor(G[:, f, a:b], SGx[:, n % 2, 0:b - a], ps[:, 2 + 2 * (n % 3), 0:b - a], ALU.mult).then_inc(s_g.sem, 1)
                s_cnt.wait(dve, 1)
                step(dve.tensor_copy(cnt[:, :], ps[:, 0, 0:E]))
                step(dve.tensor_copy(cc[:, 7:8], ps[0:E, 0, E:E + 1]))
                step(dve.tensor_scalar(cc[:, 0:6], v.cst[0:E, C_THR:C_THR + 6], cc[:, 7:8], None, ALU.is_lt))
                step(dve.tensor_reduce(cc[:, 6:7], cc[:, 0:6], AX, ALU.add))
                dve.tensor_scalar(nbb[:, :], csth[0:E, H_ONE:H_ONE + P], cc[:, 6:7], None, ALU.mult).then_inc(s_nb.sem, 1)

                def out_rows(i):
                    s_dn.wait(dve, i + 1)
                    s_ys[i % 2].wait(dve, 16 * (i // 2))
                    dve.tensor_copy(Y[:, i % 2, 512:D], ps[:, 2 + 2 * (i % 2), :]).then_inc(s_yd.sem, 1)

                out_rows(0)
                out_rows(1)
                s_slot.wait(dve, 1)
                blk = v.cst[:, C_P:C_P + 1]
                g_ps = ps[:, 7, 0:nt * E].rearrange("p (t e) -> p t e", e=E)
                step(dve.scalar_tensor_tensor(out=gm[:, :, :], in0=g_ps, scalar=1.0, in1=mr[:, :, :], op0=ALU.add, op1=ALU.mult))
                step(dve.tensor_scalar(gm[:, :, :], gm[:, :, :], -1.0, None, ALU.add))
                step(dve.scalar_tensor_tensor(out=cst128[:, :], in0=ps[:, 0, E:2 * E], scalar=float(P), in1=cnt[:, :], op0=ALU.mult, op1=ALU.add))
                step(dve.tensor_scalar(o1[:, :], ps[:, 0, 0:E], blk, None, ALU.is_le))
                step(dve.tensor_scalar(o2[:, :], ps[:, 0, E:2 * E], blk, None, ALU.is_le))
                step(dve.tensor_copy(tb[:, 3:4], ps[:, 0, E - 1:E]))
                step(dve.tensor_reduce(tb[:, 0:1], o1[:, :], AX, ALU.add))
                step(dve.tensor_tensor(o2[:, :], o2[:, :], o1[:, :], ALU.subtract))
                step(dve.tensor_tensor(o2[:, :], o2[:, :], cst128[:, :], ALU.mult))
                step(dve.tensor_reduce(tb[:, 1:2], o2[:, :], AX, ALU.add))
                step(dve.tensor_scalar(tb[:, 2:3], blk, -float(P), tb[:, 1:2], ALU.mult, ALU.add))
                step(dve.tensor_scalar(tb[:, 4:5], tb[:, 0:1], float(E - 1), None, ALU.min))
                dve.tensor_scalar(tb[:, 5:6], tb[:, 2:3], 0.0, None, ALU.max).then_inc(s_tab.sem, 1)
                out_rows(2)
                out_rows(3)
                s_tt.wait(dve, 1)
                step(dve.tensor_copy(table[0:1, 0:2 * P], ps[0:1, 0, 0:2 * P]))
                step(dve.tensor_copy(table[0:1, 2 * P:2 * P + 1], tb[0:1, 3:4]))
                for i in range(4, nt):
                    out_rows(i)
    for s, k in ((s_row, 32), (s_rw, 16), (s_sw, 48), (s_sq, nt), (s_ms, nt), (s_rstd, nt), (s_h, nt), (s_st[0], 8 * nt), (s_st[1], 8 * nt),
                 (s_t, nt), (s_ea, nt), (s_ed, nt), (s_step, counts[0]), (s_lg, 1), (s_ex, 1), (s_wt, 1), (s_ws, 16), (s_gu, len(work)),
                 (s_si, len(work)), (s_g, len(work)), (s_dn, nt), (s_ya, nt), (s_yd, nt), (s_ys[0], 8 * nt), (s_ys[1], 8 * nt),
                 (s_sel, 1), (s_cnt, 1), (s_nb, 1), (s_slot, 1), (s_tab, 1), (s_tt, 1)):
        s.stage_over(k)


def experts(v, l, nt, gm, table):
    nc, S, ps, cst, csth = v.nc, v.S, v.ps, v.cst, v.csth
    blocks = (nt * P * 8 + E * (P - 1)) // P + 1
    turns = (blocks + U - 1) // U
    assert blocks + 4 <= TABN

    def sem(n):
        return S(f"{n}_{l}").sem

    w_gu, w_d = [sem("gate_up_landed0"), sem("gate_up_landed1")], [sem("down_landed0"), sem("down_landed1")]
    listed, indexed, index, gathered = sem("slots_marked"), sem("slots_summed"), sem("index_ready"), [sem("gathered0"), sem("gathered1")]
    turned, x_act, x_dve, wcol = sem("block_turned"), sem("x_by_act"), sem("x_by_dve"), sem("weight_column")
    gate_up, silu, hidden = sem("gate_up"), sem("silu"), sem("hidden")
    down, y_act, y_dve, y_index = sem("down"), sem("y_by_act"), sem("y_by_dve"), sem("y_index")
    added, ready, step_s, cleared = sem("added"), sem("stage_ready"), sem("expert_step"), sem("cleared")
    GU_CREDIT, DOWN_CREDIT, CREDIT = 3, 2, 1
    pool_waited = sem("pool_waited")
    last_count = TABN * 2

    with ExitStack() as scope:
        def sb(n, shape, dt=F32):
            return v.sb(f"{n}_{l}", shape, dt, scope=scope)

        wgu = [sb(f"wgu{j}", [P, KD, 2 * FD]) for j in range(2)]
        wd = [sb(f"wd{j}", [P, 2, D]) for j in range(2)]
        X = [sb(f"X{j}", [P, HROW]) for j in range(2)]
        xT = sb("xT", [P, KD, P])
        SG, G = sb("SG", [P, 2, P]), sb("Gx", [P, 2, P])
        Y = [sb(f"Y{j}", [P, D]) for j in range(2)]
        cur = sb("cur", [P, nt])
        mark = sb("mark", [P, nt, P], F16)
        itmp = sb("itmp", [P, 3])
        gix = [sb(f"gix{j}", [P, 1], U32) for j in range(2)]
        six = [sb(f"six{j}", [P, 1], U32) for j in range(2)]
        wc = [sb(f"wc{j}", [P, 1]) for j in range(2)]

        def loop(eng, body):
            total = eng.value_load(table[0:1, last_count:last_count + 1], min_val=0, max_val=blocks)
            with eng.Fori(0, turns) as turn:
                with eng.If(turn * U < total):
                    for j in range(U):
                        body(turn * U + j, turn, j)

        def entry(eng, column, i, hi):
            return eng.value_load(table[0:1, bass.ds(i + column * TABN, 1)], min_val=0, max_val=hi)

        with nc.Block() as block:
            @block.sync
            def _(sp):
                def body(i, turn, j):
                    e = entry(sp, 0, i, E - 1)
                    sp.wait_ge(gate_up, i * 2 + (GU_CREDIT - 2))
                    sp.dma_start(wgu[j][:, :, :].rearrange("p k n -> p (k n)"),
                                 v.t["exp_gu"][l][bass.ds(e, 1)].rearrange("a p n -> (a p) n")).then_inc(w_gu[j], 16)
                    sp.wait_ge(down, i + (DOWN_CREDIT - 1))
                    sp.dma_start(wd[j][:, :, :].rearrange("p k n -> p (k n)"),
                                 v.t["exp_d"][l][bass.ds(e, 1)].rearrange("a p n -> (a p) n")).then_inc(w_d[j], 16)

                sp.wait_ge(ready, 1)
                loop(sp, body)

            @block.gpsimd
            def _(pool):
                def gather(j):
                    pool.indirect_dma_start(out=X[j][:, :], out_offset=None, in_=v.h2_dram,
                                            in_offset=bass.IndirectOffsetOnAxis(ap=gix[j][:, 0:1], axis=0)).then_inc(gathered[j], 16)

                def waited():
                    pool.sem_inc(pool_waited, 1)

                def body(i, turn, j):
                    pool.wait_ge(index, i + 3)
                    pool.wait_ge(turned, i + 1)
                    pool.wait_ge(wcol, i + 1)
                    waited()
                    gather(j)
                    pool.wait_ge(y_act, i + (1 + CREDIT))
                    pool.wait_ge(y_dve, i + (1 + CREDIT))
                    pool.wait_ge(y_index, i + 1)
                    pool.wait_ge(added, i * 16 + 16)
                    waited()
                    pool.indirect_dma_start(out=v.acc_dram, out_offset=bass.IndirectOffsetOnAxis(ap=six[j][:, 0:1], axis=0),
                                            in_=Y[j][:, :], in_offset=None, compute_op=ALU.add).then_inc(added, 16)
                    if j == U - 1:
                        pool.wait_ge(added, i * 16 + 32)
                        for k in range(U):
                            pool.wait_ge(gathered[k], turn * 16 + 32)

                pool.wait_ge(cleared, 3)
                pool.dma_start(v.acc_dram[NROW:NROW + P, :], Y[0][:, :]).then_inc(added, 16)
                for b in range(2):
                    pool.wait_ge(index, b + 1)
                    gather(b)
                loop(pool, body)

            @block.tensor
            def _(pe):
                def token_list(i):
                    pe.wait_ge(listed, i + 1)
                    for t in range(nt):
                        last = pe.matmul(ps[:, 2, 0:2], mark[:, t, :], csth[:, H_TOK + 2 * t:H_TOK + 2 * t + 2], start=(t == 0), stop=(t == nt - 1))
                    last.then_inc(indexed, 1)

                def turn_rows(j):
                    for k in range(KD):
                        last = pe.transpose(ps[:, 3 + k // 4, (k % 4) * P:(k % 4 + 1) * P], X[j][:, k * P:(k + 1) * P], v.ident)
                    last.then_inc(turned, 1)

                def gate_up_products(j, width):
                    for f in range(2):
                        for h in range(2):
                            for k in range(KD):
                                last = pe.matmul(ps[:, f, h * P:h * P + width], wgu[j][:, k, h * FD + f * P:h * FD + (f + 1) * P],
                                                 xT[:, k, 0:width], start=(k == 0), stop=(k == KD - 1))
                        last.then_inc(gate_up, 1)

                def body(i, turn, j):
                    n = entry(pe, 1, i, nt * P + P)
                    pe.wait_ge(w_gu[j], turn * 16 + 16)
                    pe.wait_ge(x_act, i + 1)
                    pe.wait_ge(x_dve, i + 1)
                    with pe.If(n < TIERS[0] + 1):
                        gate_up_products(j, TIERS[0])
                    with pe.Else():
                        with pe.If(n < TIERS[1] + 1):
                            gate_up_products(j, TIERS[1])
                        with pe.Else():
                            gate_up_products(j, TIERS[2])
                    pe.wait_ge(index, i + 2)
                    token_list(i + 2)
                    pe.wait_ge(gathered[(j + 1) % U], turn * 16 + (16 if j == 0 else 32))
                    turn_rows((j + 1) % U)
                    pe.wait_ge(w_d[j], turn * 16 + 16)
                    pe.wait_ge(y_act, i + CREDIT)
                    pe.wait_ge(y_dve, i + CREDIT)
                    for f in range(2):
                        pe.wait_ge(hidden, i * 2 + (f + 1 + CREDIT))
                        for c in range(2):
                            last = pe.matmul(ps[:, 5 + c, :], G[:, f, :], wd[j][:, f, c * 512:(c + 1) * 512], start=(f == 0), stop=(f == 1))
                    last.then_inc(down, 1)

                pe.wait_ge(cleared, 3)
                token_list(0)
                pe.wait_ge(index, 1)
                token_list(1)
                pe.wait_ge(gathered[0], 16)
                turn_rows(0)
                loop(pe, body)

            @block.scalar
            def _(act):
                def x_half(i):
                    act.wait_ge(turned, i + 1)
                    act.copy(xT[:, 0:4, :].rearrange("p k c -> p (k c)"), ps[:, 3, :]).then_inc(x_act, 1)

                def body(i, turn, j):
                    for f in range(2):
                        act.wait_ge(gate_up, i * 2 + (f + 1 + GU_CREDIT))
                        act.wait_ge(hidden, i * 2 + CREDIT)
                        act.activation(SG[:, f, :], ps[:, f, 0:P], ACT.Silu).then_inc(silu, 1)
                    x_half(i + 1)
                    act.wait_ge(down, i + (1 + DOWN_CREDIT))
                    act.wait_ge(added, i * 16 + 16)
                    act.wait_ge(wcol, i + 1)
                    act.activation(Y[j][:, 0:512], ps[:, 5, :], ACT.Copy, scale=wc[j][:, 0:1]).then_inc(y_act, 1)

                x_half(0)
                loop(act, body)

            @block.vector
            def _(dve):
                def mark_slots(i, e, done):
                    dve.tensor_scalar(cur[:, :], gm[:, :, bass.ds(e, 1)].rearrange("p t a -> p (t a)"),
                                      cst[:, bass.ds(i + C_NEGB, 1)], None, ALU.add).then_inc(step_s, 1)
                    dve.wait_ge(step_s, done)
                    for t in range(nt):
                        last = dve.tensor_scalar(mark[:, t, :], csth[:, H_IOTA:H_IOTA + P], cur[:, t:t + 1], None, ALU.is_equal)
                    last.then_inc(listed, 1)

                def make_index(j, done):
                    dve.tensor_copy(itmp[:, 0:2], ps[:, 2, 0:2]).then_inc(step_s, 1)
                    dve.wait_ge(step_s, done)
                    dve.scalar_tensor_tensor(out=itmp[:, 2:3], in0=itmp[:, 1:2], scalar=cst[:, C_NEGP:C_NEGP + 1], in1=itmp[:, 0:1],
                                             op0=ALU.mult, op1=ALU.add).then_inc(step_s, 1)
                    dve.wait_ge(step_s, done + 1)
                    dve.tensor_scalar(gix[j][:, :], itmp[:, 2:3], cst[:, C_TRASH:C_TRASH + 1], None, ALU.add).then_inc(index, 1)

                def x_half(i):
                    dve.wait_ge(turned, i + 1)
                    dve.tensor_copy(xT[:, 4:8, :].rearrange("p k c -> p (k c)"), ps[:, 4, :]).then_inc(x_dve, 1)

                def weight_column(e, j):
                    dve.tensor_copy(wc[j][:, :], X[j][:, bass.ds(e + D, 1)]).then_inc(wcol, 1)

                def body(i, turn, j):
                    e1, e2 = entry(dve, 0, i + 1, E - 1), entry(dve, 0, i + 2, E - 1)
                    dve.wait_ge(indexed, i + 2)
                    mark_slots(i + 2, e2, i * 3 + 7)
                    for f in range(2):
                        dve.wait_ge(silu, i * 2 + (f + 1))
                        dve.wait_ge(down, i + DOWN_CREDIT)
                        dve.tensor_tensor(G[:, f, :], SG[:, f, :], ps[:, f, P:2 * P], ALU.mult).then_inc(hidden, 1)
                    dve.wait_ge(added, i * 16 + 16)
                    dve.tensor_copy(six[j][:, :], gix[j][:, :]).then_inc(y_index, 1)
                    dve.wait_ge(y_index, i + 1)
                    dve.wait_ge(gathered[j], turn * 16 + 16)
                    dve.wait_ge(indexed, i + 3)
                    make_index(j, i * 3 + 8)
                    x_half(i + 1)
                    dve.wait_ge(y_act, i + CREDIT)
                    dve.wait_ge(y_dve, i + CREDIT)
                    weight_column(e1, (j + 1) % U)
                    dve.wait_ge(down, i + (1 + DOWN_CREDIT))
                    dve.wait_ge(wcol, i + 1)
                    dve.tensor_scalar(Y[j][:, 512:D], ps[:, 6, :], wc[j][:, 0:1], None, ALU.mult).then_inc(y_dve, 1)

                dve.memset(v.banks(0, 2), 0.0).then_inc(gate_up, GU_CREDIT)
                dve.memset(ps[:, 5, :], 0.0).then_inc(down, DOWN_CREDIT)
                dve.memset(ps[:, 6, :], 0.0).then_inc(cleared, 1)
                dve.memset(SG[:, :, :], 0.0).then_inc(ready, 1)
                dve.memset(Y[0][:, :], 0.0).then_inc(cleared, 1)
                dve.memset(G[:, :, :], 0.0).then_inc(cleared, 1)
                dve.memset(itmp[:, 0:1], 0.0).then_inc(hidden, CREDIT)
                dve.memset(itmp[:, 1:2], 0.0).then_inc(y_act, CREDIT)
                dve.memset(itmp[:, 2:3], 0.0).then_inc(y_dve, CREDIT)
                dve.wait_ge(y_dve, CREDIT)
                e = [entry(dve, 0, b, E - 1) for b in range(2)]
                mark_slots(0, e[0], 1)
                dve.wait_ge(indexed, 1)
                make_index(0, 2)
                mark_slots(1, e[1], 4)
                dve.wait_ge(indexed, 2)
                make_index(1, 5)
                x_half(0)
                weight_column(e[0], 0)
                loop(dve, body)


def ffn_residual(v, l, nt):
    nc, S = v.nc, v.S
    streams = 2 if nt == NT else 1
    s_f, s_row, s_sq, s_ms, s_rstd, s_x, s_step = (S("ffn_loaded"), S("gate_row_loaded"), S("squares"), S("mean_square"), S("rstd"),
                                                   S("x_updated"), S("dve_step"))
    counts = []
    with ExitStack() as scope:
        f = v.sb(f"f{l}", [P, nt, D], scope=scope)
        g2 = v.sb(f"g2_{l}", [P, streams, D], scope=scope)
        junk = v.sb(f"fjunk{l}", [P, D], scope=scope)
        ss = v.sb(f"fss{l}", [P, 3, NT], scope=scope)
        with nc.Block() as block:
            @block.sync
            def _(sp):
                load_rows(v, sp, g2[:, :, :], 3, streams, s_row)
                sp.dma_start(f[:, :, :], v.acc_dram[0:nt * P, :].rearrange("(t p) d -> p t d", p=P)).then_inc(s_f.sem, 16)

            @block.scalar
            def _(act):
                s_f.wait(act, 16)
                for i in range(nt):
                    s_sq.wait(act, i)
                    act.activation(junk[:, :], f[:, i, :], ACT.Square, accum_out=ss[:, 0, i:i + 1]).then_inc(s_sq.sem, 1)

            @block.gpsimd
            def _(pool):
                for i in range(nt):
                    s_ms.wait(pool, i + 1)
                    pool.tensor_tensor(ss[:, 2, i:i + 1], ss[:, 1, i:i + 1], v.half[:, 0:1], ALU.pow).then_inc(s_rstd.sem, 1)

            @block.vector
            def _(dve):
                step = stepper(dve, s_step, counts)
                s_row.wait(dve, 16)
                for i in range(nt):
                    s_sq.wait(dve, i + 1)
                    dve.tensor_scalar(ss[:, 1, i:i + 1], ss[:, 0, i:i + 1], 1.0 / D, EPS, ALU.mult, ALU.add).then_inc(s_ms.sem, 1)
                for i in range(nt):
                    s_rstd.wait(dve, i + 1)
                    step(dve.scalar_tensor_tensor(out=f[:, i, :], in0=f[:, i, :], scalar=ss[:, 2, i:i + 1],
                                                  in1=g2[:, 0 if i < LT else 1, :], op0=ALU.mult, op1=ALU.mult))
                    dve.tensor_tensor(v.xs[:, i, :], v.xs[:, i, :], f[:, i, :], ALU.add).then_inc(s_x.sem, 1)
    for s, k in ((s_f, 16), (s_row, 16), (s_sq, nt), (s_ms, nt), (s_rstd, nt), (s_x, nt), (s_step, counts[0])):
        s.stage_over(k)


def store(v):
    done = v.S("output_stored")
    with v.nc.Block() as block:
        @block.sync
        def _(sp):
            sp.dma_start(v.t["out"].rearrange("(t p) d -> p t d", p=P), v.xs[:, 0:LT, :]).then_inc(done.sem, 16)
            done.wait(sp, 16)


def constants():
    c = np.zeros((P, C_W), np.float32)
    c[:, C_ID:C_ID + P] = np.eye(P)
    tok = np.arange(SEQ)
    row, col = (tok // GRID_W).astype(np.float32), (tok % GRID_W).astype(np.float32)
    for dim, at_cos, at_sin in ((HD, C_COS, C_SIN), (32, C_COSR, C_SINR)):
        q = dim // 4
        freqs = (np.float32(10000.0) ** (-np.arange(q, dtype=np.float32) / np.float32(q))).astype(np.float32)
        ar, ac = row[:, None] * freqs, col[:, None] * freqs
        ang = np.concatenate([ar, ar, ac, ac], axis=-1).astype(np.float32)
        sign = np.repeat(np.array([-1, 1, -1, 1], np.float32), q)
        for at, tab in ((at_cos, np.cos(ang)), (at_sin, np.sin(ang) * sign)):
            c[:, at:at + LT * dim] = tab.reshape(LT, P, dim).transpose(1, 0, 2).reshape(P, LT * dim)
    q, k = np.arange(P)[:, None], np.arange(P)[None, :]
    c[:, C_PREV:C_PREV + P] = np.where(k >= q, 0, NEG)
    c[:, C_NEXT:C_NEXT + P] = np.where(k <= q, 0, NEG)
    qc, kc = (np.arange(P) % GRID_W)[:, None], np.arange(GRID_W)[None, :]
    first = np.clip(qc - 8, 0, GRID_W - 16)
    c[:, C_BAND:C_BAND + GRID_W] = np.where((kc >= first) & (kc < first + 16), 0, NEG)
    p = np.arange(P)
    c[:, C_P], c[:, C_NEGP], c[:, C_TRASH] = p, -p, NROW + p
    c[:, C_NEGB:C_NEGB + P] = -P * p[None, :]
    c[:, C_THR:C_THR + 6] = P * np.arange(6)[None, :]
    h = np.zeros((P, H_W), np.float16)
    h[:, H_TRI:H_TRI + P] = q < k
    h[:, H_ONE:H_ONE + P] = 1
    h[:, H_IOTA:H_IOTA + P] = p[None, :]
    e, f = np.arange(P)[:, None], np.arange(E)[None, :]
    h[:, H_TIN:H_TIN + E] = e <= f
    h[:, H_TST:H_TST + E] = e < f
    h[:, H_TST128:H_TST128 + E] = P * (e < f)
    for t in range(NT):
        h[:, H_TOK + 2 * t] = t * P + p - NROW
        h[:, H_TOK + 2 * t + 1] = 1
    return c, h


def layout(inp):
    f = {n: np.asarray(a) for n, a in inp.items()}
    L = DEPTH

    def cols(a):
        return a.reshape(L, -1, P).transpose(0, 2, 1)

    perm = [h * HD + i for h in SLOT_HEAD for i in range(HD)]
    order = np.arange(IN_W)
    for base in (GROUPS[0][1], GROUPS[2][1]):
        order[base:base + 256] = base + np.array(perm)
    small = np.zeros((L, P, S_W), np.float32)
    for at, n in ((S_PRE, "pre_mix_g"), (S_POST, "post_mix_g"), (S_PREF, "pre_ffn_g"), (S_POSTF, "post_ffn_g"), (S_ADAB, "ada_b")):
        c = cols(f[n])
        small[:, :, at:at + c.shape[2]] = c
    small[:, :, S_KVG] = f["b_kv_norm"]
    small[:, :, S_SINK:S_SINK + 4] = f["c_sink"][:, None, list(SLOT_HEAD)]
    for h in range(6):
        small[:, :, S_GAIN + h * HD:S_GAIN + (h + 1) * HD] = f["a_q_norm" if h < 4 else "a_k_norm"][:, None, :]
    small[:, :, S_RB:S_RB + E] = f["router_b"][:, None, :]
    dc = np.clip(np.arange(GRID_W)[None, :] - np.arange(GRID_W)[:, None] + 15, 0, 30)
    band = f["d_rpb"][:, :, :, dc].transpose(0, 3, 1, 2, 4)
    bias = np.zeros((L, P, 4, 15, GRID_W), np.float32)
    bias[:, 0:64] = band
    bias[:, 64:, :, 1:] = band[:, :, :, 0:14]
    gu = np.empty((L, E, P, KD, 2, FD), np.float32)
    gu[:, :, :, :, 0] = f["exp_w_gate"].reshape(L, E, KD, P, FD).transpose(0, 1, 3, 2, 4)
    gu[:, :, :, :, 1] = f["exp_w_up"].reshape(L, E, KD, P, FD).transpose(0, 1, 3, 2, 4)
    ed = np.ascontiguousarray(f["exp_w_down"].reshape(L, E, 2, P, D).transpose(0, 1, 3, 2, 4))
    cvec = np.stack([f["c"][0].reshape(KD, P).T, f["c_ctx"].reshape(KD, P).T], axis=2)
    consts, consts16 = constants()
    return {
        "x": f["x"][0], "ctx": f["ctx"][0], "cvec": cvec, "consts": consts, "consts16": consts16, "small": small,
        "ada_w": f["ada_w"], "w_in": f["w_in"][:, :, order], "w_up": f["b_w_kv_up"], "bias": bias, "w_out": f["w_out"],
        "router_w": f["router_w"], "sh_g": f["sh_w_gate"], "sh_u": f["sh_w_up"], "sh_d": f["sh_w_down"],
        "exp_gu": gu.reshape(L, E, P, KD * 2 * FD), "exp_d": ed.reshape(L, E, P, 2 * D),
    }


def program(nc, arrays, stop=None):
    t = {n: nc.dram_tensor("in_" + n, a.shape, mybir.dt.from_np(a.dtype), kind="ExternalInput").ap() for n, a in arrays.items()}
    t["out"] = nc.dram_tensor("out", (SEQ, D), F32, kind="ExternalOutput").ap()
    build(nc, t, stop)


def kernel(**inputs):
    import concourse.bacc as bacc
    from concourse.bass_utils import run_bass_kernel_spmd

    arrays = {n: np.ascontiguousarray(a) for n, a in layout(inputs).items()}
    nc = bacc.Bacc("TRN2", target_bir_lowering=False, num_devices=1)
    program(nc, arrays)
    r = run_bass_kernel_spmd(nc, [{"in_" + n: a for n, a in arrays.items()}], core_ids=[0])
    return r.results[0]["out"].reshape(1, SEQ, D)
```

```python
from contextlib import ExitStack

import numpy as np

import concourse.bass as bass
from concourse import mybir

F32 = mybir.dt.float32
F16 = mybir.dt.float16
I32 = mybir.dt.int32
U32 = mybir.dt.uint32
ALU = mybir.AluOpType
ACT = mybir.ActivationFunctionType
AX = mybir.AxisListType.X

P = 128
D = 1024
KD = D // P
DEPTH = 2
SEQ, CTX = 512, 256
LT, CT = SEQ // P, CTX // P
NT = LT + CT
HD = 64
GRID_W = 64
EPS = 1e-6
BIG = 3.0e38
NEG = -1e30
E = 64
NG, GE = 8, 8
TOPG = 4
FD = 256
ROUTED_SCALE = 2.5
NROW = NT * P
HROW = D + E
MAXB = (NROW * 8 + E * (P - 1)) // P + 1
TABN = P
U = 2
STRETCH = 6

GROUPS = (("A", 0, 512, 256, 0), ("B", 512, 544, 384, 256), ("C", 1056, 512, 256, 512), ("D", 1568, 768, 256, 768))
IN_W = 2336
START_COLS = 2 * D
SLOT_HEAD = (0, 2, 1, 3)

S_PRE, S_POST, S_PREF, S_POSTF, S_ADAB, S_KVG, S_SINK, S_GAIN, S_RB, S_W = 0, 8, 16, 24, 32, 80, 81, 85, 469, 533
C_ID, C_COS, C_SIN, C_COSR, C_SINR, C_PREV, C_NEXT, C_BAND, C_P, C_NEGP, C_TRASH, C_NEGB, C_THR, C_W = (
    0, 128, 384, 640, 768, 896, 1024, 1152, 1216, 1217, 1218, 1219, 1347, 1353)
H_TRI, H_ONE, H_IOTA, H_TIN, H_TST, H_TST128, H_TOK, H_W = 0, 128, 256, 384, 448, 512, 576, 588


class Signal:

    def __init__(self, sem):
        self.sem, self.base = sem, 0

    def wait(self, eng, count):
        if count > 0:
            eng.wait_ge(self.sem, self.base + count)

    def stage_over(self, total):
        self.base += total


def build(nc, t, stop=None):
    ctx = ExitStack()
    with ctx:
        signals = {}

        def S(name):
            if name not in signals:
                signals[name] = Signal(ctx.enter_context(nc.semaphore(name)))
            return signals[name]

        def sb(name, shape, dt=F32, scope=ctx):
            return scope.enter_context(nc.sbuf_tensor(name, shape, dt))

        ps = ctx.enter_context(nc.psum_tensor("ps", [P, 8, 512], F32))

        def banks(a, b):
            return ps[:, a:b, :].rearrange("p a n -> p (a n)")

        xs = sb("xs", [P, NT, D])
        cst = sb("cst", [P, C_W])
        csth = sb("csth", [P, H_W], F16)
        small = [sb(f"small{l}", [P, S_W]) for l in range(DEPTH)]
        mraw = [sb(f"mod_raw{l}", [P, 6 * KD, 2]) for l in range(DEPTH)]
        mods = sb("mods", [P, 8, 2, KD])
        csil = sb("csil", [P, KD, 2])
        half = sb("half", [P, 8])
        ones = sb("ones", [P, 1])
        ident = cst[:, C_ID:C_ID + P]

        col_dram = nc.dram_tensor("col_scratch", (64, P), F32, kind="Internal").ap()
        h2_dram = nc.dram_tensor("h2_rows", (NROW + P, HROW), F32, kind="Internal").ap()
        acc_dram = nc.dram_tensor("ffn_rows", (NROW + P, D), F32, kind="Internal").ap()

        env = dict(nc=nc, t=t, S=S, sb=sb, ps=ps, banks=banks, xs=xs, cst=cst, csth=csth, small=small, mods=mods,
                   mraw=mraw, csil=csil, half=half, ones=ones, ident=ident, col_dram=col_dram, h2_dram=h2_dram, acc_dram=acc_dram)
        env = type("Env", (), env)
        load_all(env)
        modulation_start(env)
        for l in range(DEPTH):
            nt = NT if l < DEPTH - 1 else LT
            with ExitStack() as mix:
                o_tok = sb(f"o_tok{l}", [P, nt, D], scope=mix)
                hT = sb(f"hT{l}", [P, KD, NROW], scope=mix)
                wg = [sb(f"w_in{l}_{i}", [P, KD, max(GROUPS[g][2] for g in (i, i + 2))], scope=mix) for i in range(2)]
                norm_in(env, l, hT, wg)
                for g in range(4):
                    mixer(env, l, g, nt, hT, wg, o_tok)
                project_out(env, l, nt, o_tok, wg)
            if stop == ("mix", l):
                break
            with ExitStack() as ffn:
                gm = sb(f"gm{l}", [P, nt, E], scope=ffn)
                table = sb(f"table{l}", [1, 3 * TABN + 2 + E], I32, scope=ffn)
                ex = ExpertBuffers(sb, ffn, l)
                route(env, l, nt, gm, table, ex)
                if stop == ("route", l):
                    break
                experts(env, l, nt, gm, table, ex)
            ffn_residual(env, l, nt)
            if stop == ("layer", l):
                break
        if stop:
            store(env)


class ExpertBuffers:

    def __init__(self, sb, scope, l):
        self.wgu = [sb(f"wgu0_{l}", [P, KD, 2 * FD], scope=scope)]
        self.wd = [sb(f"wd0_{l}", [P, 2, D], scope=scope)]
        self.X = [sb(f"X{j}_{l}", [P, HROW], scope=scope) for j in range(2)]
        self.Y = [sb(f"Y{j}_{l}", [P, D], scope=scope) for j in range(2)]


def load_expert(v, eng, l, e, ex):
    eng.dma_start(ex.wgu[e][:, :, :].rearrange("p k n -> p (k n)"), v.t["exp_gu"][l, e]).then_inc(v.S(f"gate_up_landed{e}_{l}").sem, 16)
    eng.dma_start(ex.wd[e][:, :, :].rearrange("p k n -> p (k n)"), v.t["exp_d"][l, e]).then_inc(v.S(f"down_landed{e}_{l}").sem, 16)


def load_all(v):
    nc, S = v.nc, v.S
    loaded, craw_loaded, silu, zero, zdone = (S("start_loaded"), S("conditioning_loaded"), S("silu_done"), S("zeroed"),
                                              S("zeros_stored"))
    with ExitStack() as scope:
        z = v.sb("zeros", [P, HROW], scope=scope)
        craw = v.sb("craw", [P, KD, 2], scope=scope)
        with nc.Block() as block:
            @block.sync
            def _(sp):
                sp.dma_start(craw[:, :, :], v.t["cvec"]).then_inc(craw_loaded.sem, 16)
                sp.dma_start(v.cst[:, :], v.t["consts"]).then_inc(loaded.sem, 16)
                sp.dma_start(v.csth[:, :], v.t["consts16"]).then_inc(loaded.sem, 16)
                for l in range(DEPTH):
                    sp.dma_start(v.small[l][:, :], v.t["small"][l]).then_inc(loaded.sem, 16)
                sp.wait_ge(loaded.sem, 64)

            @block.vector
            def _(dve):
                dve.memset(v.half[:, :], -0.5).then_inc(zero.sem, 1)
                dve.memset(v.ones[:, :], 1.0).then_inc(zero.sem, 1)
                dve.memset(z[:, :], 0.0).then_inc(zero.sem, 1)

            @block.gpsimd
            def _(pool):
                pool.wait_ge(zero.sem, 3)
                pool.dma_start(v.h2_dram[NROW:NROW + P, :], z[:, :]).then_inc(zdone.sem, 16)
                pool.wait_ge(zdone.sem, 16)

            @block.scalar
            def _(act):
                act.wait_ge(craw_loaded.sem, 16)
                act.activation(v.csil[:, :, :], craw[:, :, :], ACT.Silu).then_inc(silu.sem, 1)
    silu.stage_over(1)


def modulation_start(v):
    nc, S = v.nc, v.S
    W, nb = 2 * P, START_COLS // (2 * P)
    s_w = [S(f"ada_start_loaded{i}") for i in range(4)]
    s_mm, s_part, s_step, s_raw = S("mod_summed"), S("mod_partial"), S("dve_step"), S("mod_columns")
    s_xl = S("stream_loaded")
    counts = []
    with ExitStack() as scope:
        aw = [v.sb(f"ada_start{i}", [P, KD, W], scope=scope) for i in range(4)]
        acc = [v.sb(f"ada_part{i}", [P, 2, W], scope=scope) for i in range(2)]
        pm = v.ps[:, 0, 0:4 * nb].rearrange("p (j c) -> p j c", c=2)
        with nc.Block() as block:
            @block.sync
            def _(sp):
                for b in range(nb):
                    s_mm.wait(sp, b - 3)
                    sp.dma_start(aw[b % 4][:, :, :], v.t["ada_w"][0, :, b * W:(b + 1) * W]
                                 .rearrange("(k p) n -> p k n", p=P)).then_inc(s_w[b % 4].sem, 16)
                    if b == 3:
                        sp.dma_start(v.xs[:, 0:LT, :], v.t["x"].rearrange("(t p) d -> p t d", p=P)).then_inc(s_xl.sem, 16)
                        sp.dma_start(v.xs[:, LT:NT, :], v.t["ctx"].rearrange("(t p) d -> p t d", p=P)).then_inc(s_xl.sem, 16)
                s_xl.wait(sp, 32)

            @block.tensor
            def _(pe):
                for b in range(nb):
                    if b % 2 == 0:
                        s_w[b % 4].wait(pe, 16 * (b // 4 + 1))
                        for j in range(W // P):
                            for k in range(KD):
                                last = pe.matmul(pm[:, b * 2 + j, :], aw[b % 4][:, k, j * P:(j + 1) * P], v.csil[:, k, :],
                                                 start=(k == 0), stop=(k == KD - 1))
                    else:
                        s_part.wait(pe, b // 2 + 1)
                        for j in range(W // P):
                            for c in range(2):
                                last = pe.matmul(pm[:, b * 2 + j, c:c + 1], acc[b // 2 % 2][:, c, j * P:(j + 1) * P], v.ones[:, :],
                                                 start=True, stop=True)
                    last.then_inc(s_mm.sem, 1)

            @block.vector
            def _(dve):
                step = stepper(dve, s_step, counts)
                for b in range(1, nb, 2):
                    s_w[b % 4].wait(dve, 16 * (b // 4 + 1))
                    s_mm.wait(dve, b - 3)
                    a = acc[b // 2 % 2]
                    for k in range(KD):
                        for c in range(2):
                            if k == 0:
                                last = dve.tensor_scalar(a[:, c, :], aw[b % 4][:, k, :], v.csil[:, k, c:c + 1], None, ALU.mult)
                            else:
                                last = dve.scalar_tensor_tensor(out=a[:, c, :], in0=aw[b % 4][:, k, :], scalar=v.csil[:, k, c:c + 1],
                                                                in1=a[:, c, :], op0=ALU.mult, op1=ALU.add)
                        if k < KD - 1:
                            step(last)
                    last.then_inc(s_part.sem, 1)
                s_mm.wait(dve, nb)
                bias = v.small[0][:, S_ADAB:S_ADAB + 2 * nb].unsqueeze(2).broadcast_to([P, 2 * nb, 2])
                dve.tensor_tensor(v.mraw[0][:, 0:2 * nb, :], pm, bias, ALU.add).then_inc(s_raw.sem, 1)
    for s in s_w:
        s.stage_over(16 * (nb // 4))
    for s, k in ((s_mm, nb), (s_part, nb // 2), (s_step, counts[0]), (s_raw, 1)):
        s.stage_over(k)


def gain_columns(v, l, c):
    return v.small[l][:, c:c + KD].unsqueeze(1).broadcast_to([P, 2, KD])


def vector_columns(v, l, n):
    return v.mraw[l][:, n * KD:(n + 1) * KD, :].rearrange("p k c -> p c k")


def norm_in(v, l, hT, wg):
    nc, S, mods = v.nc, v.S, v.mods
    s_sq, s_ms, s_rstd, s_xn, s_t, s_ea, s_ed = (S("squares"), S("mean_square"), S("rstd"), S("x_normed"), S("x_turned"),
                                                 S("turned_by_act"), S("turned_by_dve"))
    s_mod, s_step = S("scale_shift_ready"), S("dve_step")
    counts = []
    with ExitStack() as scope:
        junk = v.sb(f"junk{l}", [P, D], scope=scope)
        xn = v.sb(f"xn{l}", [P, 2, D], scope=scope)
        ss = v.sb(f"ss{l}", [P, 3, NT], scope=scope)
        pt = [v.ps[:, 0:2, :], v.ps[:, 2:4, :]]
        with nc.Block() as block:
            @block.sync
            def _(sp):
                load_w_in(v, sp, l, 0, wg)

            @block.scalar
            def _(act):
                def evac(i):
                    c = 0 if i < LT else 1
                    s_t.wait(act, i + 1)
                    s_mod.wait(act, 1)
                    for k in range(4):
                        last = act.activation(hT[:, k, i * P:(i + 1) * P], pt[i % 2][:, 0, k * P:(k + 1) * P], ACT.Identity,
                                              scale=mods[:, 0, c, k:k + 1], bias=mods[:, 1, c, k:k + 1])
                    last.then_inc(s_ea.sem, 1)

                def square(i):
                    s_sq.wait(act, i)
                    act.activation(junk[:, :], v.xs[:, i, :], ACT.Square, accum_out=ss[:, 0, i:i + 1]).then_inc(s_sq.sem, 1)

                for i in range(3):
                    square(i)
                for i in range(NT):
                    if i + 3 < NT:
                        square(i + 3)
                    evac(i)

            @block.vector
            def _(dve):
                step = stepper(dve, s_step, counts)
                step(dve.tensor_copy(mods[:, 1, :, :], vector_columns(v, l, 0)))
                step(dve.tensor_scalar(mods[:, 0, :, :], vector_columns(v, l, 1), 1.0, None, ALU.add))
                dve.tensor_tensor(mods[:, 0, :, :], mods[:, 0, :, :], gain_columns(v, l, S_PRE), ALU.mult).then_inc(s_mod.sem, 1)
                s_mod.wait(dve, 1)

                def mean_square(i):
                    s_sq.wait(dve, i + 1)
                    dve.tensor_scalar(ss[:, 1, i:i + 1], ss[:, 0, i:i + 1], 1.0 / D, EPS, ALU.mult, ALU.add).then_inc(s_ms.sem, 1)

                def normed(i):
                    s_rstd.wait(dve, i + 1)
                    s_t.wait(dve, i - 1)
                    dve.tensor_scalar(xn[:, i % 2, :], v.xs[:, i, :], ss[:, 2, i:i + 1], None, ALU.mult).then_inc(s_xn.sem, 1)

                mean_square(0)
                mean_square(1)
                normed(0)
                for i in range(NT):
                    if i + 2 < NT:
                        mean_square(i + 2)
                    if i + 1 < NT:
                        normed(i + 1)
                    c = 0 if i < LT else 1
                    s_t.wait(dve, i + 1)
                    for k in range(4, 8):
                        last = dve.tensor_scalar(hT[:, k, i * P:(i + 1) * P], pt[i % 2][:, 1, (k - 4) * P:(k - 3) * P],
                                                 mods[:, 0, c, k:k + 1], mods[:, 1, c, k:k + 1], ALU.mult, ALU.add)
                    last.then_inc(s_ed.sem, 1)

            @block.gpsimd
            def _(pool):
                for i in range(NT):
                    s_ms.wait(pool, i + 1)
                    pool.tensor_tensor(ss[:, 2, i:i + 1], ss[:, 1, i:i + 1], v.half[:, 0:1], ALU.pow).then_inc(s_rstd.sem, 1)

            @block.tensor
            def _(pe):
                for i in range(NT):
                    s_xn.wait(pe, i + 1)
                    s_ea.wait(pe, i - 1)
                    s_ed.wait(pe, i - 1)
                    for k in range(KD):
                        last = pe.transpose(pt[i % 2][:, k // 4, (k % 4) * P:(k % 4 + 1) * P], xn[:, i % 2, k * P:(k + 1) * P], v.ident)
                    last.then_inc(s_t.sem, 1)
    for s in (s_sq, s_ms, s_rstd, s_xn, s_t, s_ea, s_ed):
        s.stage_over(NT)
    s_mod.stage_over(1)
    s_step.stage_over(counts[0])


def load_rows(v, eng, dst, vector, streams, signal):
    src = v.col_dram.rearrange("(v c k) p -> v c (k p)", v=4, c=2)[vector, 0:streams, :]
    eng.dma_start(dst, src.unsqueeze(0).broadcast_to([P, streams, D])).then_inc(signal.sem, 16)


def load_w_in(v, eng, l, g, wg):
    _, col, W, _, _ = GROUPS[g]
    eng.dma_start(wg[g % 2][:, :, 0:W], v.t["w_in"][l, :, col:col + W].rearrange("(k p) n -> p k n", p=P)
                  ).then_inc(v.S(f"w_in_loaded{g % 2}").sem, 16)


def load_w_out(v, eng, l, n, wg):
    eng.dma_start(wg[n][:, :, 0:512], v.t["w_out"][l, :, n * 512:(n + 1) * 512].rearrange("(k p) n -> p k n", p=P)
                  ).then_inc(v.S(f"w_out_loaded{n}").sem, 16)


def mod_pieces(l, g):
    start = START_COLS // P
    pieces = [(l, b) for b in range(start, 6 * KD)] + [(l + 1, b) for b in range(start if l + 1 < DEPTH else 0)]
    n = len(pieces) // 4
    return pieces[g * n:(g + 1) * n]


def mixer(v, l, g, nt, hT, wg, o_tok):
    nc, S, cst, small, ps = v.nc, v.S, v.cst, v.small[l], v.ps
    name, _, W, kv0, out0 = GROUPS[g]
    isA, isB, isC, isD = (name == x for x in "ABCD")
    KP = 96 if isB else P
    NQ, NK = (4, 4) if isB else (2, 2) if isD else (2, 1)
    qscale = -float((HD + 32) ** -0.5) if isB else -float(HD ** -0.5)
    has_q = [i < nt for i in range(NT)]
    nq = [sum(has_q[:i]) for i in range(NT + 1)]

    s_w = S(f"w_in_loaded{g % 2}")
    s_proj, s_v, s_rows, s_step = S("projected"), S("v_copied"), S("rows_ready"), S("dve_step")
    s_ms, s_rstd = S("head_mean_square"), S("head_rstd")
    s_t, s_qe, s_ke = S("qk_turned"), S("q_copied"), S("k_copied")
    s_cn, s_ct, s_ce, s_up, s_kn = S("latent_normed"), S("latent_turned"), S("latent_copied"), S("kv_up"), S("k_rows_copied")
    s_bias, s_band, s_wup = S("bias_loaded"), S("bias_masked"), S("w_kv_up_loaded")
    s_sc, s_max, s_exp, s_pt = S("scores"), S("negated_maximum"), S("exponentials"), S("probs_turned")
    s_pa, s_pd, s_pv, s_o, s_sx = S("probs_by_act"), S("probs_by_dve"), S("weighted_values"), S("out_written"), S("sink_exp")

    units = [(h, q) for h in range(4) for q in range(nt)]
    NU = len(units)

    def lo(u):
        q = units[u][1]
        if q >= LT:
            return 512
        if isC:
            return 512 - P * (min(q + 1, LT - 1) - max(q - 1, 0) + 1)
        return 0

    def key_tile(u, c):
        q = units[u][1]
        if c >= 4:
            return LT + c - 4
        return c - lo(u) // P + (max(q - 1, 0) if isC else 0)

    def head(slot):
        return SLOT_HEAD[slot] if isA or isC else slot

    def kv_of(slot):
        return slot % 2 if isA or isC else slot

    pieces = mod_pieces(l, g)
    NP, NA = len(pieces), 8
    unit_of = [1 + j * (NU - 2) // (NP - 1) for j in range(NP)]
    piece_of = {u: j for j, u in enumerate(unit_of)}
    assert unit_of[-1] < NU
    s_aw, s_as, s_acc = [S("ada_loaded0"), S("ada_loaded1")], S("ada_step"), S("ada_summed")
    s_mr, s_pad = S("mod_columns"), S("padded")

    steps, counts = [], []
    local = [sum(units[w][1] < LT for w in range(u + 1)) for u in range(NU)]

    with ExitStack() as scope:
        def sb(n, shape, dt=F32):
            return v.sb(f"{n}_{l}{name}", shape, dt, scope=scope)

        QT, KT, V = sb("QT", [P, 4, NROW]), sb("KT", [P, NK, NROW]), sb("V", [P, NT, 256])
        R = sb("R", [P, 2, 768])
        T1, T2, T3, T4 = (None if isD else sb(n, [P, 384]) for n in ("T1", "T2", "T3", "T4"))
        ss = sb("ss", [P, 3, NT, 8])
        if isB:
            wup = sb("wup", [P, 512])
            cn = sb("cn", [P, 2, P])
            cT = sb("cT", [P, 2, P])
        if isD:
            TD = sb("TD", [P, 4, 15, GRID_W])
        PR, PT = sb("PR", [P, 2, 768]), sb("PT", [P, 2, 768])
        nsink = sb("nsink", [P, 4])
        st = sb("st", [P, 6, NU])

        aw, tmp, acc = sb("aw", [P, 2, KD, P]), sb("atmp", [P, KD, P]), sb("aacc", [P, NA, 2, P])

        pp = [v.banks(0, 2), v.banks(2, 4)]
        tq, tk = ps[:, 4, :], ps[:, 5, :]

        with nc.Block() as block:
            @block.sync
            def _(sp):
                if isB:
                    sp.dma_start(wup[:, :], v.t["w_up"][l]).then_inc(s_wup.sem, 16)
                if isD:
                    sp.dma_start(TD[:, :, :, :], v.t["bias"][l]).then_inc(s_bias.sem, 16)
                if g < 3:
                    load_w_in(v, sp, l, g + 1, wg)
                else:
                    load_w_out(v, sp, l, 0, wg)
                for j, (ml, b) in enumerate(pieces):
                    s_acc.wait(sp, j - 1)
                    sp.dma_start(aw[:, j % 2, :, :], v.t["ada_w"][ml, :, b * P:(b + 1) * P].rearrange("(k p) n -> p k n", p=P)
                                 ).then_inc(s_aw[j % 2].sem, 16)

            @block.gpsimd
            def _(pool):
                pool_step = stepper(pool, s_as, counts)

                def piece(j):
                    s_aw[j % 2].wait(pool, 16 * (j // 2 + 1))
                    if j >= NA:
                        s_pv.wait(pool, unit_of[j - NA] + 1)
                    for c in range(2):
                        col = v.csil[:, :, c].unsqueeze(2).broadcast_to([P, KD, P])
                        pool_step(pool.tensor_tensor(tmp[:, :, :], aw[:, j % 2, :, :], col, ALU.mult))
                        for half in (4, 2):
                            pool_step(pool.tensor_tensor(tmp[:, 0:half, :], tmp[:, 0:half, :], tmp[:, half:2 * half, :], ALU.add))
                        last = pool.tensor_tensor(acc[:, j % NA, c, :], tmp[:, 0, :], tmp[:, 1, :], ALU.add)
                        if c == 0:
                            pool_step(last)
                    last.then_inc(s_acc.sem, 1)
                    s_acc.wait(pool, j + 1)

                early = 0
                if isA or isB:
                    n = 6 if isA else 1
                    for i in range(NT):
                        a = 0 if has_q[i] or isB else 4
                        s_ms.wait(pool, i + 1)
                        pool.tensor_tensor(ss[:, 2, i, a:n], ss[:, 1, i, a:n], v.half[:, a:n], ALU.pow).then_inc(s_rstd.sem, 1)
                        if 0 < i < NT - 2:
                            piece(early)
                            early += 1
                if isD:
                    s_bias.wait(pool, 16)
                    td = TD[:, :, :, :].rearrange("p h r c -> p (h r) c")
                    pool.tensor_tensor(td, td, cst[:, C_BAND:C_BAND + GRID_W].unsqueeze(1).broadcast_to([P, 60, GRID_W]),
                                       ALU.add).then_inc(s_band.sem, 1)
                for j in range(early, NP):
                    piece(j)

            @block.tensor
            def _(pe):
                def project(i):
                    s_rows.wait(pe, i - 1)
                    if not isB:
                        s_v.wait(pe, i - 1)
                    a = 0 if has_q[i] else kv0
                    for c0, c1 in ((a, min(W, 512)), (512, W)):
                        for k in range(KD if c1 > c0 else 0):
                            last = pe.matmul(pp[i % 2][:, c0:c1], hT[:, k, i * P:(i + 1) * P], wg[g % 2][:, k, c0:c1],
                                             start=(k == 0), stop=(k == KD - 1))
                    last.then_inc(s_proj.sem, 1)

                def latent(i):
                    s_cn.wait(pe, i + 1)
                    pe.transpose(ps[:, 7, 0:P], cn[:, i % 2, :], v.ident).then_inc(s_ct.sem, 1)
                    s_ce.wait(pe, i + 1)
                    s_kn.wait(pe, i)
                    pe.matmul(ps[:, 6, :], cT[:, i % 2, :], wup[:, :], start=True, stop=True).then_inc(s_up.sem, 1)

                def turn(i):
                    s_rows.wait(pe, i + 1)
                    if isB:
                        s_kn.wait(pe, i + 1)
                    s_qe.wait(pe, nq[i])
                    s_ke.wait(pe, i)
                    for j in range(0 if has_q[i] else NQ, NQ + NK):
                        dst, c = (tq, j) if j < NQ else (tk, j - NQ)
                        src = R[:, i % 2, j * KP:(j + 1) * KP]
                        last = pe.transpose(dst[0:KP, c * P:(c + 1) * P], src, v.ident)
                    last.then_inc(s_t.sem, 1)

                def scores(u):
                    s, q = units[u]
                    s_exp.wait(pe, u - 1)
                    kvp = s if isB else s // 2 if isD else 0
                    a, k0 = lo(u), key_tile(u, lo(u) // P) * P
                    lhs = QT[:, s, q * P:(q + 1) * P]
                    if a < 512:
                        pe.matmul(pp[u % 2][:, a:512], lhs, KT[:, kvp, k0:k0 + 512 - a], start=True, stop=True)
                    pe.matmul(pp[u % 2][:, 512:768], lhs, KT[:, kvp, SEQ:NROW], start=True, stop=True).then_inc(s_sc.sem, 1)

                def turn_probs(u):
                    s_exp.wait(pe, u + 1)
                    s_o.wait(pe, u - 1)
                    b = 4 + 2 * (u % 2)
                    for c in range(lo(u) // P, 6):
                        last = pe.transpose(ps[:, b + c // 4, (c % 4) * P:(c % 4 + 1) * P], PR[:, u % 2, c * P:(c + 1) * P], v.ident)
                    last.then_inc(s_pt.sem, 1)

                def values(u):
                    s_pa.wait(pe, local[u])
                    s_pd.wait(pe, u + 1)
                    c0 = kv_of(units[u][0]) * HD
                    for c in range(lo(u) // P, 6):
                        last = pe.matmul(ps[:, 5 + 2 * (u % 2), 256:256 + HD], PT[:, u % 2, c * P:(c + 1) * P],
                                         V[:, key_tile(u, c), c0:c0 + HD], start=(c == lo(u) // P), stop=(c == 5))
                    if u in piece_of:
                        j = piece_of[u]
                        s_acc.wait(pe, j + 1)
                        for c in range(2):
                            last = pe.matmul(ps[:, 5 + 2 * (u % 2), 320 + c:321 + c], acc[:, j % NA, c, :], v.ones[:, :],
                                             start=True, stop=True)
                    last.then_inc(s_pv.sem, 1)

                s_w.wait(pe, 16)
                if isB:
                    s_wup.wait(pe, 16)
                project(0)
                for i in range(NT):
                    if i + 1 < NT:
                        project(i + 1)
                    if isB:
                        latent(i)
                    turn(i)
                s_qe.wait(pe, nq[NT])
                s_ke.wait(pe, NT)
                s_pad.wait(pe, 2)
                if not isB:
                    s_v.wait(pe, NT)
                scores(0)
                for u in range(NU):
                    if u + 1 < NU:
                        scores(u + 1)
                    if u:
                        values(u - 1)
                    turn_probs(u)
                values(NU - 1)

            @block.scalar
            def _(act):
                for i in range(NT):
                    tok = slice(i * P, (i + 1) * P)
                    a = 0 if has_q[i] else kv0
                    if isA or isC:
                        s_proj.wait(act, i + 1)
                        act.copy(V[:, i, 0:P], pp[i % 2][:, 384:512]).then_inc(s_v.sem, 1)
                    if isD:
                        s_proj.wait(act, i + 1)
                        s_t.wait(act, i - 1)
                        act.copy(R[:, i % 2, a:512], pp[i % 2][:, a:512]).then_inc(s_rows.sem, 1)
                    if isB:
                        s_ct.wait(act, i + 1)
                        act.activation(cT[:, i % 2, :], ps[:, 7, 0:P], ACT.Copy, scale=small[:, S_KVG:S_KVG + 1]).then_inc(s_ce.sem, 1)
                        s_up.wait(act, i + 1)
                        s_t.wait(act, i - 1)
                        up = ps[:, 6, :].rearrange("p (h c) -> p h c", h=4)
                        act.copy(V[:, i, :].rearrange("p (h c) -> p h c", h=4), up[:, :, HD:])
                        act.copy(R[:, i % 2, :].rearrange("p (h c) -> p h c", h=8)[:, 4:8, 0:HD], up[:, :, 0:HD]).then_inc(s_kn.sem, 1)
                    if has_q[i]:
                        s_t.wait(act, i + 1)
                        src = tq[:, 0:NQ * P].rearrange("p (j c) -> p j c", j=NQ)
                        if isB:
                            last = act.mul(QT[0:KP, :, tok], src[0:KP], qscale)
                        for side in range(0 if isB else 2):
                            rows = slice(side * HD, (side + 1) * HD)
                            own = QT[rows, :, tok].rearrange("p (j s) n -> p j s n", s=2)[:, :, side, :]
                            last = act.mul(own, src[rows], qscale)
                        last.then_inc(s_qe.sem, 1)

                def exps(u):
                    s_max.wait(act, u + 1)
                    s_pt.wait(act, u - 1)
                    a = lo(u)
                    if isC:
                        act.activation(st[:, 3, u:u + 1], small[:, S_SINK + units[u][0]:S_SINK + units[u][0] + 1], ACT.Exp,
                                       bias=st[:, 1, u:u + 1])
                    act.activation(PR[:, u % 2, a:768], pp[u % 2][:, a:768], ACT.Exp, bias=st[:, 1, u:u + 1], scale=-1.0,
                                   accum_out=st[:, 2, u:u + 1]).then_inc(s_exp.sem, 1)

                exps(0)
                for u in range(NU):
                    if u + 1 < NU:
                        exps(u + 1)
                    if lo(u) < 512:
                        s_pt.wait(act, u + 1)
                        s_pv.wait(act, u - 1)
                        act.copy(PT[:, u % 2, lo(u):512], ps[:, 4 + 2 * (u % 2), lo(u):512]).then_inc(s_pa.sem, 1)

            @block.vector
            def _(dve):
                n = [0]

                def step(ins):
                    ins.then_inc(s_step.sem, 1)
                    n[0] += 1
                    s_step.wait(dve, n[0])

                def heads(ap, w=HD):
                    return ap.rearrange("p (h c) -> p h c", c=w)

                def rope(dst, src, nh, w, cos, sin, i):
                    c = cst[:, cos + i * w:cos + (i + 1) * w].unsqueeze(1).broadcast_to([P, nh, w])
                    sn = cst[:, sin + i * w:sin + (i + 1) * w].rearrange("p (a b c) -> p a b c", a=2, b=2)
                    t2 = T2[:, 0:nh * w].rearrange("p (h a b c) -> p h a b c", h=nh, a=2, b=2)
                    s4 = src.rearrange("p h (a b c) -> p h a b c", a=2, b=2)
                    for b in range(2):
                        dve.tensor_tensor(t2[:, :, :, b, :], s4[:, :, :, 1 - b, :],
                                          sn[:, :, b, :].unsqueeze(1).broadcast_to([P, nh, 2, w // 4]), ALU.mult)
                    t3 = heads(T3[:, 0:nh * w], w)
                    step(dve.tensor_tensor(t3, src, c, ALU.mult))
                    return dve.tensor_tensor(dst, t3, heads(T2[:, 0:nh * w], w), ALU.add)

                if isB:
                    dve.memset(QT[KP:P, :, :], 0.0).then_inc(s_pad.sem, 1)
                    dve.memset(KT[KP:P, :, :], 0.0).then_inc(s_pad.sem, 1)
                else:
                    for side in range(2):
                        rest = QT[(1 - side) * HD:(2 - side) * HD, :, :].rearrange("p (j s) n -> p j s n", s=2)
                        dve.memset(rest[:, :, side, :], 0.0).then_inc(s_pad.sem, 1)
                for i in range(NT):
                    tok = slice(i * P, (i + 1) * P)
                    pr = pp[i % 2]
                    s_proj.wait(dve, i + 1)
                    if isA or isC:
                        s_v.wait(dve, i + 1)
                        a = 0 if has_q[i] else 256
                        nh = (384 - a) // HD
                        src = heads(pr[:, a:384])
                        dst = heads(R[:, i % 2, a:384])
                        s_t.wait(dve, i - 1)
                    if isA:
                        h0 = a // HD
                        t1, raw = heads(T1[:, 0:nh * HD]), heads(T4[:, 0:nh * HD])
                        step(dve.tensor_copy(raw, src))
                        step(dve.tensor_tensor(t1, raw, raw, ALU.mult))
                        step(dve.tensor_reduce(ss[:, 0, i, h0:6], t1, AX, ALU.add))
                        dve.tensor_scalar(ss[:, 1, i, h0:6], ss[:, 0, i, h0:6], 1.0 / HD, EPS, ALU.mult, ALU.add).then_inc(s_ms.sem, 1)
                        s_rstd.wait(dve, i + 1)
                        step(dve.tensor_tensor(t1, raw, ss[:, 2, i, h0:6].unsqueeze(2).broadcast_to([P, nh, HD]), ALU.mult))
                        gain = heads(small[:, S_GAIN + a:S_GAIN + 384])
                        if i < LT:
                            step(dve.tensor_tensor(t1, t1, gain, ALU.mult))
                            rope(dst, t1, nh, HD, C_COS, C_SIN, i).then_inc(s_rows.sem, 1)
                        else:
                            dve.tensor_tensor(dst, t1, gain, ALU.mult).then_inc(s_rows.sem, 1)
                    elif isC:
                        if i < LT:
                            rope(dst, src, nh, HD, C_COS, C_SIN, i).then_inc(s_rows.sem, 1)
                        else:
                            dve.tensor_copy(dst, src).then_inc(s_rows.sem, 1)
                    elif isD:
                        dve.tensor_copy(V[:, i, :], pr[:, 512:768]).then_inc(s_v.sem, 1)
                    elif isB:
                        s_t.wait(dve, i - 1)
                        r8 = heads(R[:, i % 2, :], 96)
                        lat = pr[:, 384:512]
                        step(dve.tensor_copy(T4[:, 0:P], lat))
                        step(dve.tensor_tensor(T1[:, 0:P], T4[:, 0:P], T4[:, 0:P], ALU.mult))
                        step(dve.tensor_reduce(ss[:, 0, i, 0:1], T1[:, 0:P], AX, ALU.add))
                        dve.tensor_scalar(ss[:, 1, i, 0:1], ss[:, 0, i, 0:1], 1.0 / P, EPS, ALU.mult, ALU.add).then_inc(s_ms.sem, 1)
                        s_rstd.wait(dve, i + 1)
                        s_ct.wait(dve, i - 1)
                        dve.tensor_scalar(cn[:, i % 2, :], T4[:, 0:P], ss[:, 2, i, 0:1], None, ALU.mult).then_inc(s_cn.sem, 1)
                        q4 = heads(pr[:, 0:384], 96)
                        kr = pr[:, 512:544].unsqueeze(1)
                        if i < LT:
                            step(dve.tensor_copy(r8[:, 0:4, 0:HD], q4[:, :, 0:HD]))
                            step(rope(r8[:, 0:4, HD:], q4[:, :, HD:], 4, 32, C_COSR, C_SINR, i))
                            k1 = T1[:, 256:288].unsqueeze(1)
                            step(rope(k1, kr, 1, 32, C_COSR, C_SINR, i))
                            dve.tensor_copy(r8[:, 4:8, HD:], k1.broadcast_to([P, 4, 32])).then_inc(s_rows.sem, 1)
                        else:
                            if has_q[i]:
                                step(dve.tensor_copy(r8[:, 0:4, :], q4))
                            dve.tensor_copy(r8[:, 4:8, HD:], kr.broadcast_to([P, 4, 32])).then_inc(s_rows.sem, 1)
                    s_t.wait(dve, i + 1)
                    dve.tensor_copy(KT[0:KP, :, tok], tk[0:KP, 0:NK * P].rearrange("p (j c) -> p j c", j=NK)).then_inc(s_ke.sem, 1)

                def maximum(u):
                    s, q = units[u]
                    s_sc.wait(dve, u + 1)
                    sc = pp[u % 2]
                    if isD and q < LT:
                        if u == 0:
                            s_band.wait(dve, 1)
                        b = TD[:, s, 7 - 2 * q:15 - 2 * q, :].rearrange("p r c -> p (r c)")
                        step(dve.tensor_tensor(sc[:, 0:512], sc[:, 0:512], b, ALU.subtract))
                    if isC and 0 < q < LT:
                        a = lo(u)
                        step(dve.tensor_tensor(sc[:, a:a + P], sc[:, a:a + P], cst[:, C_PREV:C_PREV + P], ALU.subtract))
                    if isC and q < LT - 1:
                        step(dve.tensor_tensor(sc[:, 384:512], sc[:, 384:512], cst[:, C_NEXT:C_NEXT + P], ALU.subtract))
                    ins = dve.tensor_reduce(st[:, 0 if isC else 1, u:u + 1], sc[:, lo(u):768], AX, ALU.min)
                    if isC:
                        step(ins)
                        ins = dve.tensor_scalar(st[:, 1, u:u + 1], st[:, 0, u:u + 1], nsink[:, s:s + 1], None, ALU.min)
                    ins.then_inc(s_max.sem, 1)

                def divide(u):
                    s, q = units[u]
                    s_pv.wait(dve, u + 1)
                    den = st[:, 2, u:u + 1]
                    if isC:
                        step(dve.tensor_tensor(st[:, 4, u:u + 1], den, st[:, 3, u:u + 1], ALU.add))
                        den = st[:, 4, u:u + 1]
                    step(dve.reciprocal(st[:, 5, u:u + 1], den))
                    if u in piece_of:
                        ml, b = pieces[piece_of[u]]
                        dve.tensor_scalar(v.mraw[ml][:, b, :], ps[:, 5 + 2 * (u % 2), 320:322],
                                          v.small[ml][:, S_ADAB + b:S_ADAB + b + 1], None, ALU.add).then_inc(s_mr.sem, 1)
                    c = out0 + head(s) * HD
                    dve.tensor_scalar(o_tok[:, q, c:c + HD], ps[:, 5 + 2 * (u % 2), 256:256 + HD], st[:, 5, u:u + 1], None,
                                      ALU.mult).then_inc(s_o.sem, 1)

                if isC:
                    step(dve.tensor_scalar(nsink[:, :], small[:, S_SINK:S_SINK + 4], -1.0, None, ALU.mult))
                maximum(0)
                for u in range(NU):
                    if u + 1 < NU:
                        maximum(u + 1)
                    if u:
                        divide(u - 1)
                    s_pt.wait(dve, u + 1)
                    s_pv.wait(dve, u - 1)
                    dve.tensor_copy(PT[:, u % 2, 512:768], ps[:, 5 + 2 * (u % 2), 0:256]).then_inc(s_pd.sem, 1)
                divide(NU - 1)
                steps.append(n[0])

    steps_total = steps.pop()
    s_w.stage_over(16)
    for s, k in ((s_proj, NT), (s_rows, NT), (s_t, NT), (s_qe, nq[NT]), (s_ke, NT), (s_step, steps_total),
                 (s_sc, NU), (s_max, NU), (s_exp, NU), (s_pt, NU), (s_pa, local[-1]), (s_pd, NU), (s_pv, NU), (s_o, NU)):
        s.stage_over(k)
    for j in range(2):
        s_aw[j].stage_over(16 * ((NP + 1 - j) // 2))
    for s, k in ((s_as, counts[0]), (s_acc, NP), (s_pad, 2), (s_mr, NP)):
        s.stage_over(k)
    if not isB:
        s_v.stage_over(NT)
    if isA or isB:
        s_ms.stage_over(NT)
        s_rstd.stage_over(NT)
    if isB:
        for s, k in ((s_cn, NT), (s_ct, NT), (s_ce, NT), (s_up, NT), (s_kn, NT), (s_wup, 16)):
            s.stage_over(k)
    if isD:
        s_bias.stage_over(16)
        s_band.stage_over(1)


def stepper(dve, signal, counts):
    counts.append(0)

    def step(ins):
        ins.then_inc(signal.sem, 1)
        counts[-1] += 1
        signal.wait(dve, counts[-1])
    return step


def project_out(v, l, nt, o_tok, w):
    nc, S, ps = v.nc, v.S, v.ps
    streams = 2 if nt == NT else 1
    s_w = [S(f"w_out_loaded{n}") for n in range(2)]
    s_row, s_t, s_ea, s_ed = S("gate_row_loaded"), S("out_turned"), S("turned_by_act"), S("turned_by_dve")
    s_mm, s_sq, s_ms, s_rstd, s_x, s_step = S("mixed"), S("squares"), S("mean_square"), S("rstd"), S("x_updated"), S("dve_step")
    s_mod, s_mt, s_mc, s_cs = S("gate_columns"), S("gate_turned"), S("gate_rows"), S("gate_rows_stored")
    mods = v.mods
    counts = []
    with ExitStack() as scope:
        turned = v.sb(f"turned{l}", [64, P], scope=scope)
        g1 = v.sb(f"g1_{l}", [P, streams, D], scope=scope)
        oT = v.sb(f"oT{l}", [P, 2, KD, P], scope=scope)
        junk = v.sb(f"mjunk{l}", [P, D], scope=scope)
        add = v.sb(f"madd{l}", [P, D], scope=scope)
        ss = v.sb(f"mss{l}", [P, 3, NT], scope=scope)
        with nc.Block() as block:
            @block.sync
            def _(sp):
                load_w_out(v, sp, l, 1, w)
                s_mc.wait(sp, 1)
                sp.dma_start(v.col_dram, turned[:, :]).then_inc(s_cs.sem, 16)
                s_cs.wait(sp, 16)
                load_rows(v, sp, g1[:, :, :], 0, streams, s_row)

            @block.tensor
            def _(pe):
                def turn(i):
                    s_ea.wait(pe, i - 1)
                    s_ed.wait(pe, i - 1)
                    for k in range(KD):
                        last = pe.transpose(ps[:, 4 + 2 * (i % 2) + k // 4, (k % 4) * P:(k % 4 + 1) * P], o_tok[:, i, k * P:(k + 1) * P], v.ident)
                    last.then_inc(s_t.sem, 1)

                turn(0)
                s_mod.wait(pe, 1)
                pe.transpose(ps[0:64, 2, 0:P], mods[:, 4:8, :, :].rearrange("p v c k -> p (v c k)"), v.ident).then_inc(s_mt.sem, 1)
                for i in range(nt):
                    if i + 1 < nt:
                        turn(i + 1)
                    if i == 1:
                        s_mc.wait(pe, 1)
                    s_ea.wait(pe, i + 1)
                    s_ed.wait(pe, i + 1)
                    s_x.wait(pe, i - 1)
                    for n in range(2):
                        s_w[n].wait(pe, 16)
                        for k in range(KD):
                            last = pe.matmul(ps[:, 2 * (i % 2) + n, :], oT[:, i % 2, k, :], w[n][:, k, 0:512],
                                             start=(k == 0), stop=(k == KD - 1))
                    last.then_inc(s_mm.sem, 1)

            @block.scalar
            def _(act):
                def evac(i):
                    s_t.wait(act, i + 1)
                    s_mm.wait(act, i - 1)
                    act.copy(oT[:, i % 2, 0:4, :].rearrange("p k c -> p (k c)"), ps[:, 4 + 2 * (i % 2), :]).then_inc(s_ea.sem, 1)

                evac(0)
                for i in range(nt):
                    if i + 1 < nt:
                        evac(i + 1)
                    s_mm.wait(act, i + 1)
                    s_sq.wait(act, i)
                    act.activation(junk[:, :], v.banks(2 * (i % 2), 2 * (i % 2) + 2), ACT.Square,
                                   accum_out=ss[:, 0, i:i + 1]).then_inc(s_sq.sem, 1)

            @block.gpsimd
            def _(pool):
                for i in range(nt):
                    s_ms.wait(pool, i + 1)
                    pool.tensor_tensor(ss[:, 2, i:i + 1], ss[:, 1, i:i + 1], v.half[:, 0:1], ALU.pow).then_inc(s_rstd.sem, 1)

            @block.vector
            def _(dve):
                step = stepper(dve, s_step, counts)

                def evac(i):
                    s_t.wait(dve, i + 1)
                    s_mm.wait(dve, i - 1)
                    dve.tensor_copy(oT[:, i % 2, 4:8, :].rearrange("p k c -> p (k c)"), ps[:, 5 + 2 * (i % 2), :]).then_inc(s_ed.sem, 1)

                step(dve.tensor_tensor(mods[:, 4, :, :], vector_columns(v, l, 2), gain_columns(v, l, S_POST), ALU.mult))
                step(dve.tensor_scalar(mods[:, 5, :, :], vector_columns(v, l, 4), 1.0, None, ALU.add))
                step(dve.tensor_tensor(mods[:, 5, :, :], mods[:, 5, :, :], gain_columns(v, l, S_PREF), ALU.mult))
                step(dve.tensor_copy(mods[:, 6, :, :], vector_columns(v, l, 3)))
                dve.tensor_tensor(mods[:, 7, :, :], vector_columns(v, l, 5), gain_columns(v, l, S_POSTF), ALU.mult).then_inc(s_mod.sem, 1)
                evac(0)
                s_mt.wait(dve, 1)
                dve.tensor_copy(turned[:, :], ps[0:64, 2, 0:P]).then_inc(s_mc.sem, 1)
                for i in range(nt):
                    if i + 1 < nt:
                        evac(i + 1)
                    s_sq.wait(dve, i + 1)
                    dve.tensor_scalar(ss[:, 1, i:i + 1], ss[:, 0, i:i + 1], 1.0 / D, EPS, ALU.mult, ALU.add).then_inc(s_ms.sem, 1)
                    s_rstd.wait(dve, i + 1)
                    s_x.wait(dve, i)
                    s_row.wait(dve, 16)
                    step(dve.scalar_tensor_tensor(out=add[:, :], in0=v.banks(2 * (i % 2), 2 * (i % 2) + 2), scalar=ss[:, 2, i:i + 1],
                                                  in1=g1[:, 0 if i < LT else 1, :], op0=ALU.mult, op1=ALU.mult))
                    dve.tensor_tensor(v.xs[:, i, :], v.xs[:, i, :], add[:, :], ALU.add).then_inc(s_x.sem, 1)
    for s, k in ((s_w[0], 16), (s_w[1], 16), (s_row, 16), (s_t, nt), (s_ea, nt), (s_ed, nt), (s_mm, nt), (s_sq, nt), (s_ms, nt), (s_rstd, nt),
                 (s_x, nt), (s_step, counts[0]), (s_mod, 1), (s_mt, 1), (s_mc, 1), (s_cs, 16)):
        s.stage_over(k)


def route(v, l, nt, gm, table, ex):
    nc, S, ps, small, csth = v.nc, v.S, v.ps, v.small[l], v.csth
    streams = 2 if nt == NT else 1
    NTOK = nt * P
    pieces = [(0, 512)] + ([(512, 768)] if nt == NT else [])
    work = [(f, a, b) for a, b in pieces for f in range(2)]
    s_row, s_rw, s_sw = S("ffn_rows_loaded"), S("router_loaded"), S("shared_loaded")
    s_sq, s_ms, s_rstd, s_h = S("squares"), S("mean_square"), S("rstd"), S("h2_ready")
    s_st = [S("h2_stored0"), S("h2_stored1")]
    s_t, s_ea, s_ed, s_step = S("h2_turned"), S("turned_by_act"), S("turned_by_dve"), S("dve_step")
    s_lg, s_ex, s_wt, s_ws = S("logits"), S("logits_exp"), S("weights_ready"), S("weights_stored")
    s_clear = S("cleared")
    s_gu, s_si, s_g = S("shared_gate_up"), S("shared_silu"), S("shared_hidden")
    s_dn, s_ya, s_yd = S("shared_down"), S("shared_by_act"), S("shared_by_dve")
    s_ys = [S("shared_stored0"), S("shared_stored1")]
    s_sel, s_cnt, s_nb, s_slot, s_tab, s_tt = S("chosen"), S("counted"), S("blocks_counted"), S("slots"), S("table_columns"), S("table_turned")
    counts = []
    with ExitStack() as scope:
        def sb(n, shape, dt=F32):
            return v.sb(f"{n}_{l}", shape, dt, scope=scope)

        ab = sb("ab", [P, 2, streams, D])
        rw = sb("rw", [P, KD, E])
        sgu = sb("sgu", [P, KD, 2, FD])
        sd = sb("sd", [P, 2, D])
        H = sb("H", [P, 2, D])
        hT = sb("h2T", [P, KD, NTOK])
        junk = sb("rjunk", [P, D])
        ss = sb("rss", [P, 3, NT])
        SGx = sb("SGx", [P, 2, 512])
        G = sb("G", [P, 2, NTOK])
        Y = sb("Ysh", [P, 2, D])
        exps, sc, sbv, cand, mr, w = (sb(n, [P, nt, E]) for n in ("ex", "sc", "sbv", "cand", "mr", "wts"))
        sel = sb("sel", [P, nt, E], F16)
        g8, m8, rp, i12, o12 = sb("g8", [P, nt, NG, 8]), sb("m8", [P, nt, 8]), sb("rp", [P, nt, 8]), sb("i12", [P, nt, 12]), sb("o12", [P, nt, 12])
        gk, pen, wsum = sb("gk", [P, nt, NG]), sb("pen", [P, nt, NG]), sb("wsum", [P, 2, nt])
        cc = sb("cc", [E, 8])
        nbb = sb("nbb", [E, P], F16)
        o1 = sb("o1", [P, E])
        tb = sb("tb", [P, 7])

        with nc.Block() as block:
            @block.sync
            def _(sp):
                for r in range(2):
                    load_rows(v, sp, ab[:, r, :, :], 1 + r, streams, s_row)
                sp.dma_start(rw[:, :, :], v.t["router_w"][l].rearrange("(k p) n -> p k n", p=P)).then_inc(s_rw.sem, 16)
                for i in range(nt):
                    s_h.wait(sp, i + 1)
                    sp.dma_start(v.h2_dram[i * P:(i + 1) * P, 0:D], H[:, i % 2, :]).then_inc(s_st[i % 2].sem, 16)
                    if i == 0:
                        sp.dma_start(sgu[:, :, 0, :], v.t["sh_g"][l].rearrange("(k p) n -> p k n", p=P)).then_inc(s_sw.sem, 16)
                    if i == 1:
                        sp.dma_start(sgu[:, :, 1, :], v.t["sh_u"][l].rearrange("(k p) n -> p k n", p=P)).then_inc(s_sw.sem, 16)
                    if i == 2:
                        sp.dma_start(sd[:, :, :], v.t["sh_d"][l].rearrange("(f p) n -> p f n", p=P)).then_inc(s_sw.sem, 16)
                load_expert(v, sp, l, 0, ex)
                s_wt.wait(sp, 1)
                sp.dma_start(v.h2_dram[0:NTOK, D:HROW].rearrange("(t p) e -> p t e", p=P), w[:, :, :]).then_inc(s_ws.sem, 16)
                for i in range(nt):
                    s_ya.wait(sp, i + 1)
                    s_yd.wait(sp, i + 1)
                    sp.dma_start(v.acc_dram[i * P:(i + 1) * P, :], Y[:, i % 2, :]).then_inc(s_ys[i % 2].sem, 16)
                for j in range(2):
                    s_st[j].wait(sp, 16 * (nt // 2))
                    s_ys[j].wait(sp, 16 * (nt // 2))
                s_ws.wait(sp, 16)

            @block.gpsimd
            def _(pool):
                for n, a in enumerate((ex.X[0][:, :], ex.X[1][:, :], ex.Y[0][:, :])):
                    pool.memset(a, 0.0).then_inc(s_clear.sem, 1)
                    s_clear.wait(pool, n + 1)
                for i in range(nt):
                    s_ms.wait(pool, i + 1)
                    pool.tensor_tensor(ss[:, 2, i:i + 1], ss[:, 1, i:i + 1], v.half[:, 0:1], ALU.pow).then_inc(s_rstd.sem, 1)

            @block.tensor
            def _(pe):
                for i in range(nt):
                    s_h.wait(pe, i + 1)
                    s_ea.wait(pe, i - 1)
                    s_ed.wait(pe, i - 1)
                    for k in range(KD):
                        last = pe.transpose(ps[:, 4 + 2 * (i % 2) + k // 4, (k % 4) * P:(k % 4 + 1) * P], H[:, i % 2, k * P:(k + 1) * P], v.ident)
                    last.then_inc(s_t.sem, 1)
                s_ea.wait(pe, nt)
                s_ed.wait(pe, nt)
                s_rw.wait(pe, 16)
                for i in range(nt):
                    for k in range(KD):
                        last = pe.matmul(ps[:, 0, i * E:(i + 1) * E], hT[:, k, i * P:(i + 1) * P], rw[:, k, :], start=(k == 0), stop=(k == KD - 1))
                last.then_inc(s_lg.sem, 1)
                s_sw.wait(pe, 48)
                for n, (f, a, b) in enumerate(work):
                    s_g.wait(pe, n - 2)
                    for h in range(2):
                        for k in range(KD):
                            last = pe.matmul(ps[:, 1 + 2 * (n % 3) + h, 0:b - a], sgu[:, k, h, f * P:(f + 1) * P], hT[:, k, a:b],
                                             start=(k == 0), stop=(k == KD - 1))
                    last.then_inc(s_gu.sem, 1)
                s_ex.wait(pe, 1)
                s_sel.wait(pe, 1)
                ones = csth[:, H_ONE:H_ONE + P]
                for i in range(nt):
                    last = pe.matmul(ps[0:E, 0, E:E + 1], sel[:, i, :], ones[:, 0:1], start=(i == 0), stop=(i == nt - 1))
                last.then_inc(s_cnt.sem, 1)

                def down(i):
                    s_g.wait(pe, len(work))
                    s_ya.wait(pe, i - 1)
                    s_yd.wait(pe, i - 1)
                    for n in range(2):
                        for f in range(2):
                            last = pe.matmul(ps[:, 1 + 2 * (i % 2) + n, :], G[:, f, i * P:(i + 1) * P], sd[:, f, n * 512:(n + 1) * 512],
                                             start=(f == 0), stop=(f == 1))
                    last.then_inc(s_dn.sem, 1)

                down(0)
                down(1)
                s_nb.wait(pe, 1)
                pe.matmul(ps[:, 0, 0:E], nbb[:, :], csth[0:E, H_TIN:H_TIN + E], start=True, stop=True)
                for i in range(nt):
                    out = ps[:, 7, i * E:(i + 1) * E]
                    pe.matmul(out, nbb[:, :], csth[0:E, H_TST128:H_TST128 + E], start=True, stop=False)
                    for j in range(i):
                        pe.matmul(out, ones, sel[:, j, :], start=False, stop=False)
                    last = pe.matmul(out, csth[:, H_TRI:H_TRI + P], sel[:, i, :], start=False, stop=True)
                last.then_inc(s_slot.sem, 1)
                down(2)
                down(3)
                s_tab.wait(pe, 1)
                for c in range(3):
                    last = pe.matmul(ps[0:1, 0, c * P:(c + 1) * P], tb[:, 3 + c:4 + c], v.ident, start=True, stop=True)
                last.then_inc(s_tt.sem, 1)
                for i in range(4, nt):
                    down(i)

            @block.scalar
            def _(act):
                for i in range(nt):
                    s_sq.wait(act, i)
                    act.activation(junk[:, :], v.xs[:, i, :], ACT.Square, accum_out=ss[:, 0, i:i + 1]).then_inc(s_sq.sem, 1)
                for i in range(nt):
                    s_t.wait(act, i + 1)
                    act.copy(hT[:, 0:4, i * P:(i + 1) * P], ps[:, 4 + 2 * (i % 2), :].rearrange("p (k c) -> p k c", k=4)).then_inc(s_ea.sem, 1)
                s_lg.wait(act, 1)
                act.activation(exps[:, :, :].rearrange("p t e -> p (t e)"), ps[:, 0, 0:nt * E], ACT.Exp, scale=-1.0).then_inc(s_ex.sem, 1)
                for n, (f, a, b) in enumerate(work):
                    s_gu.wait(act, n + 1)
                    s_g.wait(act, n - 1)
                    act.activation(SGx[:, n % 2, 0:b - a], ps[:, 1 + 2 * (n % 3), 0:b - a], ACT.Silu).then_inc(s_si.sem, 1)
                for i in range(nt):
                    s_dn.wait(act, i + 1)
                    s_ys[i % 2].wait(act, 16 * (i // 2))
                    act.copy(Y[:, i % 2, 0:512], ps[:, 1 + 2 * (i % 2), :]).then_inc(s_ya.sem, 1)

            @block.vector
            def _(dve):
                step = stepper(dve, s_step, counts)

                def mean_square(i):
                    s_sq.wait(dve, i + 1)
                    dve.tensor_scalar(ss[:, 1, i:i + 1], ss[:, 0, i:i + 1], 1.0 / D, EPS, ALU.mult, ALU.add).then_inc(s_ms.sem, 1)

                mean_square(0)
                mean_square(1)
                s_row.wait(dve, 32)

                def h2(i):
                    if i + 2 < nt:
                        mean_square(i + 2)
                    c = 0 if i < LT else 1
                    s_rstd.wait(dve, i + 1)
                    s_t.wait(dve, i - 1)
                    s_st[i % 2].wait(dve, 16 * (i // 2))
                    step(dve.scalar_tensor_tensor(out=H[:, i % 2, :], in0=v.xs[:, i, :], scalar=ss[:, 2, i:i + 1], in1=ab[:, 0, c, :],
                                                  op0=ALU.mult, op1=ALU.mult))
                    dve.tensor_tensor(H[:, i % 2, :], H[:, i % 2, :], ab[:, 1, c, :], ALU.add).then_inc(s_h.sem, 1)

                h2(0)
                for i in range(nt):
                    if i + 1 < nt:
                        h2(i + 1)
                    s_t.wait(dve, i + 1)
                    dve.tensor_copy(hT[:, 4:8, i * P:(i + 1) * P], ps[:, 5 + 2 * (i % 2), :].rearrange("p (k c) -> p k c", k=4)).then_inc(s_ed.sem, 1)
                s_ex.wait(dve, 1)
                rb = small[:, S_RB:S_RB + E].unsqueeze(1).broadcast_to([P, nt, E])
                step(dve.tensor_scalar(exps[:, :, :], exps[:, :, :], 1.0, None, ALU.add))
                step(dve.reciprocal(sc[:, :, :], exps[:, :, :]))
                step(dve.tensor_tensor(sbv[:, :, :], sc[:, :, :], rb, ALU.add))
                for i in range(nt):
                    for g in range(NG):
                        dve.max(g8[:, i, g, :], sbv[:, i, g * GE:(g + 1) * GE])
                dve.memset(i12[:, :, 8:12], -BIG)
                step(dve.memset(rp[:, :, TOPG:8], -BIG))
                step(dve.tensor_tensor(i12[:, :, 0:8], g8[:, :, :, 0], g8[:, :, :, 1], ALU.add))
                for i in range(nt):
                    last = dve.max(m8[:, i, :], i12[:, i, 0:8])
                step(last)
                step(dve.tensor_copy(rp[:, :, 0:TOPG], m8[:, :, 0:TOPG]))
                for i in range(nt):
                    last = dve.match_replace(o12[:, i, :], rp[:, i, :], i12[:, i, :], BIG)
                step(last)
                step(dve.tensor_scalar(gk[:, :, :], o12[:, :, 0:8], BIG, None, ALU.is_equal))
                step(dve.tensor_scalar(pen[:, :, :], gk[:, :, :], -1.0, BIG, ALU.add, ALU.mult))

                def by_group(a):
                    return a.rearrange("p t (g e) -> p (t g) e", g=NG)

                def over_group(a):
                    return a.rearrange("p t g -> p (t g)").unsqueeze(2).broadcast_to([P, nt * NG, GE])

                step(dve.tensor_tensor(by_group(cand[:, :, :]), by_group(sbv[:, :, :]), over_group(gk[:, :, :]), ALU.mult))
                step(dve.tensor_tensor(by_group(cand[:, :, :]), by_group(cand[:, :, :]), over_group(pen[:, :, :]), ALU.add))
                for i in range(nt):
                    last = dve.max(m8[:, i, :], cand[:, i, :])
                step(last)
                for i in range(nt):
                    last = dve.match_replace(mr[:, i, :], m8[:, i, :], cand[:, i, :], BIG)
                step(last)
                dve.tensor_scalar(sel[:, :, :], mr[:, :, :], BIG, None, ALU.is_equal).then_inc(s_sel.sem, 1)
                step(dve.tensor_scalar(mr[:, :, :], mr[:, :, :], BIG, None, ALU.is_equal))
                step(dve.tensor_tensor(w[:, :, :], sc[:, :, :], mr[:, :, :], ALU.mult))
                step(dve.tensor_reduce(wsum[:, 0, :], w[:, :, :], AX, ALU.add))
                step(dve.reciprocal(wsum[:, 1, :], wsum[:, 0, :]))
                dve.scalar_tensor_tensor(out=w[:, :, :], in0=w[:, :, :], scalar=ROUTED_SCALE, in1=wsum[:, 1, :].unsqueeze(2).broadcast_to([P, nt, E]),
                                         op0=ALU.mult, op1=ALU.mult).then_inc(s_wt.sem, 1)
                for n, (f, a, b) in enumerate(work):
                    s_si.wait(dve, n + 1)
                    dve.tensor_tensor(G[:, f, a:b], SGx[:, n % 2, 0:b - a], ps[:, 2 + 2 * (n % 3), 0:b - a], ALU.mult).then_inc(s_g.sem, 1)
                s_cnt.wait(dve, 1)
                step(dve.tensor_copy(cc[:, 7:8], ps[0:E, 0, E:E + 1]))
                step(dve.tensor_scalar(cc[:, 0:6], v.cst[0:E, C_THR:C_THR + 6], cc[:, 7:8], None, ALU.is_lt))
                step(dve.tensor_reduce(cc[:, 6:7], cc[:, 0:6], AX, ALU.add))
                dve.tensor_scalar(nbb[:, :], csth[0:E, H_ONE:H_ONE + P], cc[:, 6:7], None, ALU.mult).then_inc(s_nb.sem, 1)

                def out_rows(i):
                    s_dn.wait(dve, i + 1)
                    s_ys[i % 2].wait(dve, 16 * (i // 2))
                    dve.tensor_copy(Y[:, i % 2, 512:D], ps[:, 2 + 2 * (i % 2), :]).then_inc(s_yd.sem, 1)

                out_rows(0)
                out_rows(1)
                s_slot.wait(dve, 1)
                blk = v.cst[:, C_P:C_P + 1]
                g_ps = ps[:, 7, 0:nt * E].rearrange("p (t e) -> p t e", e=E)
                step(dve.scalar_tensor_tensor(out=gm[:, :, :], in0=g_ps, scalar=1.0, in1=mr[:, :, :], op0=ALU.add, op1=ALU.mult))
                step(dve.tensor_scalar(gm[:, :, :], gm[:, :, :], -1.0, None, ALU.add))
                step(dve.tensor_scalar(o1[:, :], ps[:, 0, 0:E], blk, None, ALU.is_le))
                step(dve.tensor_copy(tb[:, 1:2], ps[:, 0, E - 1:E]))
                step(dve.tensor_reduce(tb[:, 0:1], o1[:, :], AX, ALU.add))
                step(dve.tensor_scalar(tb[:, 6:7], tb[:, 1:2], 0.5, 0.25, ALU.mult, ALU.add))
                step(dve.tensor_scalar(tb[:, 6:7], tb[:, 6:7], 12582912.0, None, ALU.add))
                step(dve.tensor_scalar(tb[:, 6:7], tb[:, 6:7], -12582912.0, None, ALU.add))
                step(dve.tensor_scalar(tb[:, 6:7], tb[:, 6:7], 16.0, None, ALU.mult))
                step(dve.tensor_scalar(tb[:, 3:4], tb[:, 0:1], float(E - 1), None, ALU.min))
                step(dve.tensor_scalar(tb[:, 2:3], tb[:, 3:4], 0.5, -0.25, ALU.mult, ALU.add))
                step(dve.tensor_scalar(tb[:, 2:3], tb[:, 2:3], 12582912.0, None, ALU.add))
                step(dve.tensor_scalar(tb[:, 2:3], tb[:, 2:3], -12582912.0, None, ALU.add))
                step(dve.tensor_scalar(tb[:, 4:5], tb[:, 2:3], -2.0, tb[:, 3:4], ALU.mult, ALU.add))
                step(dve.memset(table[0:1, 3 * P + 1:3 * P + 3], 0))
                step(dve.tensor_copy(table[0:1, 3 * P + 3:3 * P + 1 + E], ps[0:1, 0, 0:E - 2]))
                dve.tensor_scalar(tb[:, 5:6], tb[:, 2:3], 16.0, 16.0, ALU.mult, ALU.add).then_inc(s_tab.sem, 1)
                out_rows(2)
                out_rows(3)
                s_tt.wait(dve, 1)
                step(dve.tensor_copy(table[0:1, 0:3 * P], ps[0:1, 0, 0:3 * P]))
                step(dve.tensor_copy(table[0:1, 3 * P:3 * P + 1], tb[0:1, 1:2]))
                step(dve.tensor_copy(table[0:1, 3 * P + 1 + E:3 * P + 2 + E], tb[0:1, 6:7]))
                for i in range(4, nt):
                    out_rows(i)
    for s, k in ((s_row, 32), (s_rw, 16), (s_sw, 48), (s_sq, nt), (s_ms, nt), (s_rstd, nt), (s_h, nt), (s_st[0], 8 * nt), (s_st[1], 8 * nt),
                 (s_t, nt), (s_ea, nt), (s_ed, nt), (s_step, counts[0]), (s_lg, 1), (s_ex, 1), (s_wt, 1), (s_ws, 16), (s_gu, len(work)),
                 (s_si, len(work)), (s_g, len(work)), (s_dn, nt), (s_ya, nt), (s_yd, nt), (s_ys[0], 8 * nt), (s_ys[1], 8 * nt),
                 (s_clear, 3), (s_sel, 1), (s_cnt, 1), (s_nb, 1), (s_slot, 1), (s_tab, 1), (s_tt, 1)):
        s.stage_over(k)


def experts(v, l, nt, gm, table, ex):
    nc, S, ps, cst, csth = v.nc, v.S, v.ps, v.cst, v.csth
    blocks = (nt * P * 8 + E * (P - 1)) // P + 1
    turns = (blocks + U - 1) // U
    assert -(-turns // STRETCH) * STRETCH * U + 2 <= TABN

    def sem(n):
        return S(f"{n}_{l}").sem

    w_gu, w_d = [sem("gate_up_landed0"), sem("gate_up_landed1")], [sem("down_landed0"), sem("down_landed1")]
    listed, indexed, index, gathered = sem("slots_marked"), sem("slots_summed"), sem("index_ready"), [sem("gathered0"), sem("gathered1")]
    turned, x_act, x_dve, wcol = sem("block_turned"), sem("x_by_act"), sem("x_by_dve"), sem("weight_column")
    gate_up, silu, hidden = sem("gate_up"), sem("silu"), sem("hidden")
    down, y_act, y_dve, y_index = sem("down"), sem("y_by_act"), sem("y_by_dve"), sem("y_index")
    added, step_s = sem("added"), sem("expert_step")
    GU_CREDIT, DOWN_CREDIT, CREDIT = 1, 1, 1
    pool_waited = sem("pool_waited")
    last_count = TABN * 3

    with ExitStack() as scope:
        def sb(n, shape, dt=F32):
            return v.sb(f"{n}_{l}", shape, dt, scope=scope)

        ex.wgu.append(sb("wgu1", [P, KD, 2 * FD]))
        ex.wd.append(sb("wd1", [P, 2, D]))
        wgu, wd, X, Y = ex.wgu, ex.wd, ex.X, ex.Y
        SG, G = sb("silu", [P, 2, P]), sb("hidden", [P, 2, P])
        xT = sb("xT", [P, KD, P])
        cur = sb("cur", [P, nt])
        mark = sb("mark", [P, nt, P], F16)
        itmp = sb("itmp", [P, 3])
        gix = [sb(f"gix{j}", [P, 1], U32) for j in range(2)]
        six = [sb(f"six{j}", [P, 1], U32) for j in range(2)]
        wc = [sb(f"wc{j}", [P, 1]) for j in range(2)]

        def loop(eng, body):
            total = eng.value_load(table[0:1, last_count:last_count + 1], min_val=0, max_val=blocks)
            with eng.Fori(0, -(-turns // STRETCH)) as stretch:
                with eng.If(stretch * (STRETCH * U) < total):
                    with eng.Fori(0, STRETCH) as k:
                        turn = eng.snap(stretch * STRETCH + k)
                        with eng.If(turn * U < total):
                            for j in range(U):
                                body(turn * U + j, turn, j)

        def entry(eng, column, i, hi):
            return eng.value_load(table[0:1, bass.ds(i + column * TABN, 1)], min_val=0, max_val=hi)

        with nc.Block() as block:
            @block.sync
            def _(sp):
                sp.wait_ge(index, 2)
                load_expert(v, sp, l, 1, ex)
                with sp.Fori(1, E // 2) as pair:
                    for w in range(2):
                        e = pair * 2 + w
                        before = sp.value_load(table[0:1, bass.ds(e + (last_count + 1), 1)], min_val=0, max_val=blocks)
                        sp.wait_ge(gate_up, before * 2 + GU_CREDIT)
                        sp.dma_start(wgu[w][:, :, :].rearrange("p k n -> p (k n)"),
                                     v.t["exp_gu"][l][bass.ds(e, 1)].rearrange("a p n -> (a p) n")).then_inc(w_gu[w], 16)
                        sp.wait_ge(down, before + DOWN_CREDIT)
                        sp.dma_start(wd[w][:, :, :].rearrange("p k n -> p (k n)"),
                                     v.t["exp_d"][l][bass.ds(e, 1)].rearrange("a p n -> (a p) n")).then_inc(w_d[w], 16)

            @block.gpsimd
            def _(pool):
                def gather(j):
                    pool.indirect_dma_start(out=X[j][:, :], out_offset=None, in_=v.h2_dram,
                                            in_offset=bass.IndirectOffsetOnAxis(ap=gix[j][:, 0:1], axis=0),
                                            bounds_check=NROW - 1, oob_is_err=False).then_inc(gathered[j], 16)

                def waited():
                    pool.sem_inc(pool_waited, 1)

                def body(i, turn, j):
                    pool.wait_ge(index, i + 3)
                    pool.wait_ge(turned, i + 1)
                    pool.wait_ge(wcol, i + 1)
                    waited()
                    gather(j)
                    pool.wait_ge(y_act, i + (1 + CREDIT))
                    pool.wait_ge(y_dve, i + (1 + CREDIT))
                    pool.wait_ge(y_index, i + 1)
                    pool.wait_ge(added, i * 16 + 16)
                    waited()
                    pool.indirect_dma_start(out=v.acc_dram, out_offset=bass.IndirectOffsetOnAxis(ap=six[j][:, 0:1], axis=0),
                                            in_=Y[j][:, :], in_offset=None, compute_op=ALU.add).then_inc(added, 16)

                pool.dma_start(v.acc_dram[NROW:NROW + P, :], Y[0][:, :]).then_inc(added, 16)
                for b in range(2):
                    pool.wait_ge(index, b + 1)
                    gather(b)
                loop(pool, body)
                turns16 = pool.value_load(table[0:1, last_count + 1 + E:last_count + 2 + E], min_val=0, max_val=turns * 16)
                pool.wait_ge(added, turns16 * 2 + 16)
                for k in range(U):
                    pool.wait_ge(gathered[k], turns16 + 16)

            @block.tensor
            def _(pe):
                def token_list(i):
                    pe.wait_ge(listed, i + 1)
                    for t in range(nt):
                        last = pe.matmul(ps[:, 2, 0:2], mark[:, t, :], csth[:, H_TOK + 2 * t:H_TOK + 2 * t + 2], start=(t == 0), stop=(t == nt - 1))
                    last.then_inc(indexed, 1)

                def turn_rows(j):
                    for k in range(KD):
                        last = pe.transpose(ps[:, 3 + k // 4, (k % 4) * P:(k % 4 + 1) * P], X[j][:, k * P:(k + 1) * P], v.ident)
                    last.then_inc(turned, 1)

                def gate_up_products(w):
                    for f in range(2):
                        for h in range(2):
                            for k in range(KD):
                                last = pe.matmul(ps[:, f, h * P:(h + 1) * P], wgu[w][:, k, h * FD + f * P:h * FD + (f + 1) * P],
                                                 xT[:, k, :], start=(k == 0), stop=(k == KD - 1))
                        last.then_inc(gate_up, 1)

                def down_products(w):
                    for f in range(2):
                        for c in range(2):
                            last = pe.matmul(ps[:, 5 + c, :], G[:, f, :], wd[w][:, f, c * 512:(c + 1) * 512], start=(f == 0), stop=(f == 1))
                    last.then_inc(down, 1)

                def body(i, turn, j):
                    odd = entry(pe, 1, i, 1)
                    landed = entry(pe, 2, i, E // 2 * 16)
                    pe.wait_ge(x_act, i + 1)
                    pe.wait_ge(x_dve, i + 1)
                    with pe.If(odd < 1):
                        pe.wait_ge(w_gu[0], landed)
                        gate_up_products(0)
                    with pe.Else():
                        pe.wait_ge(w_gu[1], landed)
                        gate_up_products(1)
                    pe.wait_ge(index, i + 2)
                    token_list(i + 2)
                    pe.wait_ge(gathered[(j + 1) % U], turn * 16 + (16 if j == 0 else 32))
                    turn_rows((j + 1) % U)
                    pe.wait_ge(y_act, i + CREDIT)
                    pe.wait_ge(y_dve, i + CREDIT)
                    pe.wait_ge(hidden, i * 2 + (2 + CREDIT))
                    with pe.If(odd < 1):
                        pe.wait_ge(w_d[0], landed)
                        down_products(0)
                    with pe.Else():
                        pe.wait_ge(w_d[1], landed)
                        down_products(1)

                token_list(0)
                pe.wait_ge(index, 1)
                token_list(1)
                pe.wait_ge(gathered[0], 16)
                turn_rows(0)
                loop(pe, body)

            @block.scalar
            def _(act):
                def x_half(i):
                    act.wait_ge(turned, i + 1)
                    act.copy(xT[:, 0:4, :].rearrange("p k c -> p (k c)"), ps[:, 3, :]).then_inc(x_act, 1)

                def body(i, turn, j):
                    for f in range(2):
                        act.wait_ge(gate_up, i * 2 + (f + 1 + GU_CREDIT))
                        act.wait_ge(hidden, i * 2 + CREDIT)
                        act.activation(SG[:, f, :], ps[:, f, 0:P], ACT.Silu).then_inc(silu, 1)
                    x_half(i + 1)
                    act.wait_ge(down, i + (1 + DOWN_CREDIT))
                    act.wait_ge(added, i * 16 + 16)
                    act.wait_ge(wcol, i + 1)
                    act.activation(Y[j][:, 0:512], ps[:, 5, :], ACT.Copy, scale=wc[j][:, 0:1]).then_inc(y_act, 1)

                x_half(0)
                loop(act, body)

            @block.vector
            def _(dve):
                def mark_slots(i, e, done):
                    dve.tensor_scalar(cur[:, :], gm[:, :, bass.ds(e, 1)].rearrange("p t a -> p (t a)"),
                                      cst[:, bass.ds(i + C_NEGB, 1)], None, ALU.add).then_inc(step_s, 1)
                    dve.wait_ge(step_s, done)
                    for t in range(nt):
                        last = dve.tensor_scalar(mark[:, t, :], csth[:, H_IOTA:H_IOTA + P], cur[:, t:t + 1], None, ALU.is_equal)
                    last.then_inc(listed, 1)

                def make_index(j, done):
                    dve.tensor_copy(itmp[:, 0:2], ps[:, 2, 0:2]).then_inc(step_s, 1)
                    dve.wait_ge(step_s, done)
                    dve.scalar_tensor_tensor(out=itmp[:, 2:3], in0=itmp[:, 1:2], scalar=cst[:, C_NEGP:C_NEGP + 1], in1=itmp[:, 0:1],
                                             op0=ALU.mult, op1=ALU.add).then_inc(step_s, 1)
                    dve.wait_ge(step_s, done + 1)
                    dve.tensor_scalar(gix[j][:, :], itmp[:, 2:3], cst[:, C_TRASH:C_TRASH + 1], None, ALU.add).then_inc(index, 1)

                def x_half(i):
                    dve.wait_ge(turned, i + 1)
                    dve.tensor_copy(xT[:, 4:8, :].rearrange("p k c -> p (k c)"), ps[:, 4, :]).then_inc(x_dve, 1)

                def weight_column(e, j):
                    dve.tensor_copy(wc[j][:, :], X[j][:, bass.ds(e + D, 1)]).then_inc(wcol, 1)

                def body(i, turn, j):
                    e1, e2 = entry(dve, 0, i + 1, E - 1), entry(dve, 0, i + 2, E - 1)
                    dve.wait_ge(indexed, i + 2)
                    mark_slots(i + 2, e2, i * 3 + 7)
                    for f in range(2):
                        dve.wait_ge(silu, i * 2 + (f + 1))
                        dve.wait_ge(down, i + DOWN_CREDIT)
                        dve.tensor_tensor(G[:, f, :], SG[:, f, :], ps[:, f, P:2 * P], ALU.mult).then_inc(hidden, 1)
                    dve.wait_ge(added, i * 16 + 16)
                    dve.tensor_copy(six[j][:, :], gix[j][:, :]).then_inc(y_index, 1)
                    dve.wait_ge(y_index, i + 1)
                    dve.wait_ge(gathered[j], turn * 16 + 16)
                    dve.wait_ge(indexed, i + 3)
                    make_index(j, i * 3 + 8)
                    x_half(i + 1)
                    dve.wait_ge(y_act, i + CREDIT)
                    dve.wait_ge(y_dve, i + CREDIT)
                    weight_column(e1, (j + 1) % U)
                    dve.wait_ge(down, i + (1 + DOWN_CREDIT))
                    dve.wait_ge(wcol, i + 1)
                    dve.tensor_scalar(Y[j][:, 512:D], ps[:, 6, :], wc[j][:, 0:1], None, ALU.mult).then_inc(y_dve, 1)

                dve.memset(wc[0][:, :], 0.0).then_inc(gate_up, GU_CREDIT)
                dve.memset(wc[1][:, :], 0.0).then_inc(down, DOWN_CREDIT)
                dve.memset(itmp[:, 0:1], 0.0).then_inc(hidden, CREDIT)
                dve.memset(itmp[:, 1:2], 0.0).then_inc(y_act, CREDIT)
                dve.memset(itmp[:, 2:3], 0.0).then_inc(y_dve, CREDIT)
                dve.wait_ge(y_dve, CREDIT)
                e = [entry(dve, 0, b, E - 1) for b in range(2)]
                mark_slots(0, e[0], 1)
                dve.wait_ge(indexed, 1)
                make_index(0, 2)
                mark_slots(1, e[1], 4)
                dve.wait_ge(indexed, 2)
                make_index(1, 5)
                x_half(0)
                weight_column(e[0], 0)
                loop(dve, body)


def ffn_residual(v, l, nt):
    nc, S = v.nc, v.S
    streams = 2 if nt == NT else 1
    s_row, s_sq, s_ms, s_rstd, s_x, s_step = (S("gate_row_loaded"), S("squares"), S("mean_square"), S("rstd"),
                                              S("x_updated"), S("dve_step"))
    s_f = [S(f"ffn_loaded{i}") for i in range(nt)]
    done = S("output_stored")
    counts = []
    with ExitStack() as scope:
        f = v.sb(f"f{l}", [P, nt, D], scope=scope)
        g2 = v.sb(f"g2_{l}", [P, streams, D], scope=scope)
        junk = v.sb(f"fjunk{l}", [P, D], scope=scope)
        ss = v.sb(f"fss{l}", [P, 3, NT], scope=scope)
        with nc.Block() as block:
            @block.sync
            def _(sp):
                for i in range(nt):
                    sp.dma_start(f[:, i, :], v.acc_dram[i * P:(i + 1) * P, :]).then_inc(s_f[i].sem, 16)
                    if i == 0:
                        load_rows(v, sp, g2[:, :, :], 3, streams, s_row)
                if l == DEPTH - 1:
                    for i in range(nt):
                        s_x.wait(sp, i + 1)
                        sp.dma_start(v.t["out"][i * P:(i + 1) * P, :], v.xs[:, i, :]).then_inc(done.sem, 16)
                    done.wait(sp, 16 * nt)

            @block.scalar
            def _(act):
                for i in range(nt):
                    s_f[i].wait(act, 16)
                    s_sq.wait(act, i)
                    act.activation(junk[:, :], f[:, i, :], ACT.Square, accum_out=ss[:, 0, i:i + 1]).then_inc(s_sq.sem, 1)

            @block.gpsimd
            def _(pool):
                for i in range(nt):
                    s_ms.wait(pool, i + 1)
                    pool.tensor_tensor(ss[:, 2, i:i + 1], ss[:, 1, i:i + 1], v.half[:, 0:1], ALU.pow).then_inc(s_rstd.sem, 1)

            @block.vector
            def _(dve):
                step = stepper(dve, s_step, counts)

                def mean_square(i):
                    s_sq.wait(dve, i + 1)
                    dve.tensor_scalar(ss[:, 1, i:i + 1], ss[:, 0, i:i + 1], 1.0 / D, EPS, ALU.mult, ALU.add).then_inc(s_ms.sem, 1)

                mean_square(0)
                s_row.wait(dve, 16)
                for i in range(nt):
                    if i + 1 < nt:
                        mean_square(i + 1)
                    s_rstd.wait(dve, i + 1)
                    step(dve.scalar_tensor_tensor(out=f[:, i, :], in0=f[:, i, :], scalar=ss[:, 2, i:i + 1],
                                                  in1=g2[:, 0 if i < LT else 1, :], op0=ALU.mult, op1=ALU.mult))
                    dve.tensor_tensor(v.xs[:, i, :], v.xs[:, i, :], f[:, i, :], ALU.add).then_inc(s_x.sem, 1)
    for s in s_f:
        s.stage_over(16)
    for s, k in ((s_row, 16), (s_sq, nt), (s_ms, nt), (s_rstd, nt), (s_x, nt), (s_step, counts[0])):
        s.stage_over(k)


def store(v):
    done = v.S("output_stored")
    with v.nc.Block() as block:
        @block.sync
        def _(sp):
            sp.dma_start(v.t["out"].rearrange("(t p) d -> p t d", p=P), v.xs[:, 0:LT, :]).then_inc(done.sem, 16)
            done.wait(sp, 16)


def constants():
    c = np.zeros((P, C_W), np.float32)
    c[:, C_ID:C_ID + P] = np.eye(P)
    tok = np.arange(SEQ)
    row, col = (tok // GRID_W).astype(np.float32), (tok % GRID_W).astype(np.float32)
    for dim, at_cos, at_sin in ((HD, C_COS, C_SIN), (32, C_COSR, C_SINR)):
        q = dim // 4
        freqs = (np.float32(10000.0) ** (-np.arange(q, dtype=np.float32) / np.float32(q))).astype(np.float32)
        ar, ac = row[:, None] * freqs, col[:, None] * freqs
        ang = np.concatenate([ar, ar, ac, ac], axis=-1).astype(np.float32)
        sign = np.repeat(np.array([-1, 1, -1, 1], np.float32), q)
        for at, tab in ((at_cos, np.cos(ang)), (at_sin, np.sin(ang) * sign)):
            c[:, at:at + LT * dim] = tab.reshape(LT, P, dim).transpose(1, 0, 2).reshape(P, LT * dim)
    q, k = np.arange(P)[:, None], np.arange(P)[None, :]
    c[:, C_PREV:C_PREV + P] = np.where(k >= q, 0, NEG)
    c[:, C_NEXT:C_NEXT + P] = np.where(k <= q, 0, NEG)
    qc, kc = (np.arange(P) % GRID_W)[:, None], np.arange(GRID_W)[None, :]
    first = np.clip(qc - 8, 0, GRID_W - 16)
    c[:, C_BAND:C_BAND + GRID_W] = np.where((kc >= first) & (kc < first + 16), 0, NEG)
    p = np.arange(P)
    c[:, C_P], c[:, C_NEGP], c[:, C_TRASH] = p, -p, NROW + p
    c[:, C_NEGB:C_NEGB + P] = -P * p[None, :]
    c[:, C_THR:C_THR + 6] = P * np.arange(6)[None, :]
    c[:, C_THR] = -1
    h = np.zeros((P, H_W), np.float16)
    h[:, H_TRI:H_TRI + P] = q < k
    h[:, H_ONE:H_ONE + P] = 1
    h[:, H_IOTA:H_IOTA + P] = p[None, :]
    e, f = np.arange(P)[:, None], np.arange(E)[None, :]
    h[:, H_TIN:H_TIN + E] = e <= f
    h[:, H_TST:H_TST + E] = e < f
    h[:, H_TST128:H_TST128 + E] = P * (e < f)
    for t in range(NT):
        h[:, H_TOK + 2 * t] = t * P + p - NROW
        h[:, H_TOK + 2 * t + 1] = 1
    return c, h


def layout(inp):
    f = {n: np.asarray(a) for n, a in inp.items()}
    L = DEPTH

    def cols(a):
        return a.reshape(L, -1, P).transpose(0, 2, 1)

    perm = [h * HD + i for h in SLOT_HEAD for i in range(HD)]
    order = np.arange(IN_W)
    for base in (GROUPS[0][1], GROUPS[2][1]):
        order[base:base + 256] = base + np.array(perm)
    small = np.zeros((L, P, S_W), np.float32)
    for at, n in ((S_PRE, "pre_mix_g"), (S_POST, "post_mix_g"), (S_PREF, "pre_ffn_g"), (S_POSTF, "post_ffn_g"), (S_ADAB, "ada_b")):
        c = cols(f[n])
        small[:, :, at:at + c.shape[2]] = c
    small[:, :, S_KVG] = f["b_kv_norm"]
    small[:, :, S_SINK:S_SINK + 4] = f["c_sink"][:, None, list(SLOT_HEAD)]
    for h in range(6):
        small[:, :, S_GAIN + h * HD:S_GAIN + (h + 1) * HD] = f["a_q_norm" if h < 4 else "a_k_norm"][:, None, :]
    small[:, :, S_RB:S_RB + E] = f["router_b"][:, None, :]
    dc = np.clip(np.arange(GRID_W)[None, :] - np.arange(GRID_W)[:, None] + 15, 0, 30)
    band = f["d_rpb"][:, :, :, dc].transpose(0, 3, 1, 2, 4)
    bias = np.zeros((L, P, 4, 15, GRID_W), np.float32)
    bias[:, 0:64] = band
    bias[:, 64:, :, 1:] = band[:, :, :, 0:14]
    gu = np.empty((L, E, P, KD, 2, FD), np.float32)
    gu[:, :, :, :, 0] = f["exp_w_gate"].reshape(L, E, KD, P, FD).transpose(0, 1, 3, 2, 4)
    gu[:, :, :, :, 1] = f["exp_w_up"].reshape(L, E, KD, P, FD).transpose(0, 1, 3, 2, 4)
    ed = np.ascontiguousarray(f["exp_w_down"].reshape(L, E, 2, P, D).transpose(0, 1, 3, 2, 4))
    cvec = np.stack([f["c"][0].reshape(KD, P).T, f["c_ctx"].reshape(KD, P).T], axis=2)
    consts, consts16 = constants()
    return {
        "x": f["x"][0], "ctx": f["ctx"][0], "cvec": cvec, "consts": consts, "consts16": consts16, "small": small,
        "ada_w": f["ada_w"], "w_in": f["w_in"][:, :, order], "w_up": f["b_w_kv_up"], "bias": bias, "w_out": f["w_out"],
        "router_w": f["router_w"], "sh_g": f["sh_w_gate"], "sh_u": f["sh_w_up"], "sh_d": f["sh_w_down"],
        "exp_gu": gu.reshape(L, E, P, KD * 2 * FD), "exp_d": ed.reshape(L, E, P, 2 * D),
    }


def program(nc, arrays, stop=None):
    t = {n: nc.dram_tensor("in_" + n, a.shape, mybir.dt.from_np(a.dtype), kind="ExternalInput").ap() for n, a in arrays.items()}
    t["out"] = nc.dram_tensor("out", (SEQ, D), F32, kind="ExternalOutput").ap()
    build(nc, t, stop)


def kernel(**inputs):
    import concourse.bacc as bacc
    from concourse.bass_utils import run_bass_kernel_spmd

    arrays = {n: np.ascontiguousarray(a) for n, a in layout(inputs).items()}
    nc = bacc.Bacc("TRN2", target_bir_lowering=False, num_devices=1)
    program(nc, arrays)
    r = run_bass_kernel_spmd(nc, [{"in_" + n: a for n, a in arrays.items()}], core_ids=[0])
    return r.results[0]["out"].reshape(1, SEQ, D)
```
